# Optimizing a Trainium2 kernel written in Bass

```python
import math
import jax, jax.numpy as jnp
from jax import lax
import numpy as np

D_MODEL = 1024
BATCH = 1
SEQ = 512
DEPTH = 2
DEC_BATCH = 8
DEC_SEQ = 8
PAST_LEN = 4096
PAGE_SIZE = 128

H_RET = 4
DK_RET = 128
DV_RET = 128
RET_W = H_RET * DV_RET
ROPE_BASE = 10000.0
H_SSD = 16
P_SSD = 64
G_SSD = 2
N_SSD = 64
R_SSD = H_SSD // G_SSD
SSD_W = H_SSD * P_SSD
CONV_K = 4
CONV_DIM = SSD_W + 2 * G_SSD * N_SSD
CHUNK = 128
N_EGROUPS = 4
EXP_PER_GROUP = 4
N_EXPERTS = N_EGROUPS * EXP_PER_GROUP
TOP_K = 2
D_FF = 512
EPS = 1e-6
IN_SIZES = [RET_W, RET_W, RET_W, RET_W, SSD_W, CONV_DIM, H_SSD, D_MODEL, D_MODEL]
IN_COLS = sum(IN_SIZES)

kernel_name = 'retnet_mamba2_hmoe_step'

def rmsnorm(x, g):
    xf = x.astype(jnp.float32)
    r = lax.rsqrt(jnp.mean(xf * xf, axis=-1, keepdims=True) + EPS)
    return (xf * r * g.astype(jnp.float32)).astype(x.dtype)

def rotary(x, pos):
    half = x.shape[-1] // 2
    inv = ROPE_BASE ** (-jnp.arange(half, dtype=jnp.float32) / half)
    ang = pos[:, None] * inv[None, :]
    c = jnp.cos(ang)[None, :, None, :]
    s = jnp.sin(ang)[None, :, None, :]
    x1, x2 = x[..., :half], x[..., half:]
    return jnp.concatenate([x1 * c - x2 * s, x2 * c + x1 * s], axis=-1)

def to_chunks(t, c):
    b, l = t.shape[:2]
    return jnp.moveaxis(t.reshape((b, l // c, c) + t.shape[2:]), 1, 0)

def from_chunks(t):
    nc, b, c = t.shape[:3]
    return jnp.moveaxis(t, 0, 1).reshape((b, nc * c) + t.shape[3:])

def retention(q, k, v, s0):
    l = q.shape[1]
    c = math.gcd(l, CHUNK)
    log_g = jnp.log1p(-jnp.exp2(-5.0 - jnp.arange(H_RET, dtype=jnp.float32)))
    idx = jnp.arange(c, dtype=jnp.float32)
    rel = idx[:, None] - idx[None, :]
    causal = rel >= 0
    dmat = jnp.where(causal[None], jnp.exp(jnp.where(causal, rel, 0.0)[None] * log_g[:, None, None]), 0.0)
    q_dec = jnp.exp((idx[:, None] + 1.0) * log_g[None, :])[None, :, :, None]
    k_dec = jnp.exp((c - 1.0 - idx[:, None]) * log_g[None, :])[None, :, :, None]
    chunk_dec = jnp.exp(c * log_g)[None, :, None, None]

    def step(s, inp):
        qc, kc, vc = inp
        sc = jnp.einsum('bnhd,bmhd->bhnm', qc, kc) * dmat
        o = jnp.einsum('bhnm,bmhv->bnhv', sc, vc) + jnp.einsum('bnhd,bhdv->bnhv', qc, s) * q_dec
        s = chunk_dec * s + jnp.einsum('bmhd,bmhv->bhdv', kc * k_dec, vc)
        return s, o

    s, o = lax.scan(step, s0, (to_chunks(q, c), to_chunks(k, c), to_chunks(v, c)))
    return from_chunks(o), s

def ssd(x, dt, bm, cm, a, s0):
    l = x.shape[1]
    c = math.gcd(l, CHUNK)
    mask = jnp.tril(jnp.ones((c, c), dtype=bool))[None, :, :, None, None]

    def step(s, inp):
        xc, dtc, bc, cc = inp
        cum = jnp.cumsum(dtc * a, axis=1)
        seg = cum[:, :, None] - cum[:, None, :]
        lmat = jnp.exp(jnp.where(mask, seg, -jnp.inf))
        cb = jnp.einsum('bngk,bmgk->bnmg', cc, bc)
        w = lmat * cb[..., None] * dtc[:, None]
        y = jnp.einsum('bnmgr,bmgrp->bngrp', w, xc)
        y = y + jnp.exp(cum)[..., None] * jnp.einsum('bngk,bgrpk->bngrp', cc, s)
        wend = jnp.exp(cum[:, -1:] - cum) * dtc
        s = jnp.exp(cum[:, -1])[..., None, None] * s + jnp.einsum('bmgr,bmgrp,bmgk->bgrpk', wend, xc, bc)
        return s, y

    s, y = lax.scan(step, s0, (to_chunks(x, c), to_chunks(dt, c), to_chunks(bm, c), to_chunks(cm, c)))
    return from_chunks(y), s

def hier_moe(h, w_rg, w_re, w_gate, w_up, w_down):
    b, l, d = h.shape
    t = h.reshape(-1, d)
    n_tok = t.shape[0]
    glog = (t @ w_rg).astype(jnp.float32)
    gprob = jax.nn.softmax(glog, axis=-1)
    gidx = jnp.argmax(glog, axis=-1)
    gw = jnp.take_along_axis(gprob, gidx[:, None], axis=-1)[:, 0]
    elog = (t @ w_re).astype(jnp.float32).reshape(n_tok, N_EGROUPS, EXP_PER_GROUP)
    sel = jnp.take_along_axis(elog, gidx[:, None, None], axis=1)[:, 0]
    top_v, top_i = lax.top_k(sel, TOP_K)
    wts = jax.nn.softmax(top_v, axis=-1) * gw[:, None]
    flat_e = (gidx[:, None] * EXP_PER_GROUP + top_i).reshape(-1)
    flat_w = wts.reshape(-1)
    order = jnp.argsort(flat_e)
    tok = order // TOP_K
    gs = jnp.bincount(flat_e, length=N_EXPERTS).astype(jnp.int32)
    xs = t[tok]
    act = jax.nn.silu(lax.ragged_dot(xs, w_gate, gs)) * lax.ragged_dot(xs, w_up, gs)
    out = lax.ragged_dot(act, w_down, gs) * flat_w[order][:, None].astype(t.dtype)
    y = jnp.zeros_like(t).at[tok].add(out)
    return y.reshape(b, l, d)

def layer(x, pos, s_ret, s_ssm, s_conv, ln1_g, w_in, ret_gn_g, w_ret_out, conv_w, conv_b,
          dt_bias, a_log, d_skip, ssd_norm_g, w_ssd_out, w_o, ln2_g, w_rg, w_re, w_gate, w_up, w_down):
    b, l, _ = x.shape
    f32 = jnp.float32
    h = rmsnorm(x, ln1_g)
    proj = h @ w_in
    splits = [int(v) for v in np.cumsum(IN_SIZES)[:-1]]
    q, k, v, rg, z, xbc, dt_raw, g_ret, g_ssd = jnp.split(proj, splits, axis=-1)

    q = rotary(q.reshape(b, l, H_RET, DK_RET).astype(f32), pos)
    k = rotary(k.reshape(b, l, H_RET, DK_RET).astype(f32), pos) * (DK_RET ** -0.5)
    v = v.reshape(b, l, H_RET, DV_RET).astype(f32)
    o, s_ret_new = retention(q, k, v, s_ret.astype(f32))
    mu = jnp.mean(o, axis=-1, keepdims=True)
    var = jnp.mean(jnp.square(o - mu), axis=-1, keepdims=True)
    on = ((o - mu) * lax.rsqrt(var + EPS)).reshape(b, l, RET_W) * ret_gn_g.astype(f32)
    ret_y = (jax.nn.silu(rg.astype(f32)) * on).astype(x.dtype) @ w_ret_out

    xpad = jnp.concatenate([s_conv.astype(xbc.dtype), xbc], axis=1)
    conv = conv_b.astype(f32) + sum(xpad[:, j:j + l].astype(f32) * conv_w[j].astype(f32) for j in range(CONV_K))
    conv = jax.nn.silu(conv)
    new_conv = xpad[:, xpad.shape[1] - (CONV_K - 1):]
    xs, bm, cm = jnp.split(conv, [SSD_W, SSD_W + G_SSD * N_SSD], axis=-1)
    xs = xs.reshape(b, l, G_SSD, R_SSD, P_SSD)
    dt = jax.nn.softplus(dt_raw.astype(f32) + dt_bias.astype(f32)).reshape(b, l, G_SSD, R_SSD)
    a = -jnp.exp(a_log.astype(f32)).reshape(G_SSD, R_SSD)
    y, s_ssm_new = ssd(xs, dt, bm.reshape(b, l, G_SSD, N_SSD), cm.reshape(b, l, G_SSD, N_SSD), a,
                       s_ssm.astype(f32).reshape(b, G_SSD, R_SSD, P_SSD, N_SSD))
    y = y + d_skip.astype(f32).reshape(G_SSD, R_SSD)[..., None] * xs
    y = (y.reshape(b, l, SSD_W) * jax.nn.silu(z.astype(f32))).reshape(b, l, G_SSD, SSD_W // G_SSD)
    y = y * lax.rsqrt(jnp.mean(y * y, axis=-1, keepdims=True) + EPS)
    y = y.reshape(b, l, SSD_W) * ssd_norm_g.astype(f32)
    ssd_y = y.astype(x.dtype) @ w_ssd_out

    m = jax.nn.sigmoid(g_ret) * ret_y + jax.nn.sigmoid(g_ssd) * ssd_y
    x = x + m @ w_o
    x = x + hier_moe(rmsnorm(x, ln2_g), w_rg, w_re, w_gate, w_up, w_down)
    return (x, s_ret_new.astype(x.dtype),
            s_ssm_new.reshape(b, H_SSD, P_SSD, N_SSD).astype(x.dtype), new_conv.astype(x.dtype))

def trunk(x, start, s_ret, s_ssm, s_conv, ln1_g, w_in, ret_gn_g, w_ret_out, conv_w, conv_b,
          dt_bias, a_log, d_skip, ssd_norm_g, w_ssd_out, w_o, ln2_g, w_rg, w_re, w_gate, w_up,
          w_down, lnf_g):
    pos = start + jnp.arange(x.shape[1], dtype=jnp.float32)
    rets, ssms, convs = [], [], []
    for i in range(DEPTH):
        x, r, s, c = layer(x, pos, s_ret[i], s_ssm[i], s_conv[i], ln1_g[i], w_in[i], ret_gn_g[i],
                           w_ret_out[i], conv_w[i], conv_b[i], dt_bias[i], a_log[i], d_skip[i],
                           ssd_norm_g[i], w_ssd_out[i], w_o[i], ln2_g[i], w_rg[i], w_re[i],
                           w_gate[i], w_up[i], w_down[i])
        rets.append(r)
        ssms.append(s)
        convs.append(c)
    return rmsnorm(x, lnf_g), jnp.stack(rets), jnp.stack(ssms), jnp.stack(convs)

def setup_inputs(seed: int = 0) -> dict:
    key = jax.random.key(seed)
    ks = jax.random.split(key, 26)
    nrm = jax.random.normal
    f32 = jnp.float32
    dt0 = jnp.exp(jax.random.uniform(ks[10], (DEPTH, H_SSD), f32, math.log(1e-3), math.log(1e-1)))
    return {
        'x_prompt': nrm(ks[0], (BATCH, SEQ, D_MODEL), f32),
        'x_sample': nrm(ks[1], (DEC_BATCH, DEC_SEQ, D_MODEL), f32),
        'state_ret': 0.1 * nrm(ks[2], (DEPTH, DEC_BATCH, H_RET, DK_RET, DV_RET), f32),
        'state_ssm': 0.1 * nrm(ks[3], (DEPTH, DEC_BATCH, H_SSD, P_SSD, N_SSD), f32),
        'state_conv': nrm(ks[4], (DEPTH, DEC_BATCH, CONV_K - 1, CONV_DIM), f32),
        'ln1_g': 1.0 + 0.02 * nrm(ks[5], (DEPTH, D_MODEL), f32),
        'w_in': nrm(ks[6], (DEPTH, D_MODEL, IN_COLS), f32) * D_MODEL ** -0.5,
        'ret_gn_g': 1.0 + 0.02 * nrm(ks[7], (DEPTH, RET_W), f32),
        'w_ret_out': nrm(ks[8], (DEPTH, RET_W, D_MODEL), f32) * RET_W ** -0.5,
        'conv_w': nrm(ks[9], (DEPTH, CONV_K, CONV_DIM), f32) * CONV_K ** -0.5,
        'conv_b': 0.02 * nrm(ks[11], (DEPTH, CONV_DIM), f32),
        'dt_bias': dt0 + jnp.log(-jnp.expm1(-dt0)),
        'a_log': jnp.log(jax.random.uniform(ks[12], (DEPTH, H_SSD), f32, 1.0, 16.0)),
        'd_skip': 1.0 + 0.02 * nrm(ks[13], (DEPTH, H_SSD), f32),
        'ssd_norm_g': 1.0 + 0.02 * nrm(ks[14], (DEPTH, SSD_W), f32),
        'w_ssd_out': nrm(ks[15], (DEPTH, SSD_W, D_MODEL), f32) * SSD_W ** -0.5,
        'w_o': nrm(ks[16], (DEPTH, D_MODEL, D_MODEL), f32) * D_MODEL ** -0.5,
        'ln2_g': 1.0 + 0.02 * nrm(ks[17], (DEPTH, D_MODEL), f32),
        'w_router_group': nrm(ks[18], (DEPTH, D_MODEL, N_EGROUPS), f32) * D_MODEL ** -0.5,
        'w_router_expert': nrm(ks[19], (DEPTH, D_MODEL, N_EXPERTS), f32) * D_MODEL ** -0.5,
        'w_e_gate': nrm(ks[20], (DEPTH, N_EXPERTS, D_MODEL, D_FF), f32) * D_MODEL ** -0.5,
        'w_e_up': nrm(ks[21], (DEPTH, N_EXPERTS, D_MODEL, D_FF), f32) * D_MODEL ** -0.5,
        'w_e_down': nrm(ks[22], (DEPTH, N_EXPERTS, D_FF, D_MODEL), f32) * D_FF ** -0.5,
        'lnf_g': 1.0 + 0.02 * nrm(ks[23], (D_MODEL,), f32),
    }

def reference(x_prompt, x_sample, state_ret, state_ssm, state_conv, ln1_g, w_in, ret_gn_g, w_ret_out,
              conv_w, conv_b, dt_bias, a_log, d_skip, ssd_norm_g, w_ssd_out, w_o, ln2_g,
              w_router_group, w_router_expert, w_e_gate, w_e_up, w_e_down, lnf_g):
    dt = x_prompt.dtype
    z_ret = jnp.zeros((DEPTH, BATCH, H_RET, DK_RET, DV_RET), dt)
    z_ssm = jnp.zeros((DEPTH, BATCH, H_SSD, P_SSD, N_SSD), dt)
    z_conv = jnp.zeros((DEPTH, BATCH, CONV_K - 1, CONV_DIM), dt)
    y_prompt, p_ret, p_ssm, p_conv = trunk(
        x_prompt, 0.0, z_ret, z_ssm, z_conv, ln1_g, w_in, ret_gn_g, w_ret_out, conv_w, conv_b,
        dt_bias, a_log, d_skip, ssd_norm_g, w_ssd_out, w_o, ln2_g, w_router_group, w_router_expert,
        w_e_gate, w_e_up, w_e_down, lnf_g)
    y_sample, s_ret, s_ssm, s_conv = trunk(
        x_sample, float(PAST_LEN), state_ret, state_ssm, state_conv, ln1_g, w_in, ret_gn_g, w_ret_out,
        conv_w, conv_b, dt_bias, a_log, d_skip, ssd_norm_g, w_ssd_out, w_o, ln2_g, w_router_group,
        w_router_expert, w_e_gate, w_e_up, w_e_down, lnf_g)
    return (y_prompt, y_sample, p_ret, p_ssm, p_conv, s_ret, s_ssm, s_conv)


_drawn_inputs = setup_inputs


def setup_inputs(seed=0):
    import zlib

    import numpy as np

    out = dict(_drawn_inputs(seed))
    spreads = {}
    factors = {}
    for name, (base, spread) in spreads.items():
        noise = np.random.default_rng([zlib.crc32(name.encode()), seed]).standard_normal(out[name].shape)
        drawn = base * np.exp(spread * noise) if base else spread * noise
        out[name] = __import__('jax').numpy.asarray(drawn.astype(out[name].dtype))
    for name, factor in factors.items():
        out[name] = (out[name] * factor).astype(out[name].dtype)
    return out
```

```python
from contextlib import ExitStack

import numpy as np

import concourse.bass as bass
from concourse import mybir

F32 = mybir.dt.float32
BF16 = mybir.dt.bfloat16
I32 = mybir.dt.int32
ALU = mybir.AluOpType
ACT = mybir.ActivationFunctionType
AX = mybir.AxisListType

P = 128
DEPTH, D_MODEL = 2, 1024
SEQ, DEC_B, DEC_S, PAST = 512, 8, 8, 4096
NSAMP = DEC_B * DEC_S
TOK = SEQ + NSAMP
NT = SEQ // P + 1
SAMPLE = NT - 1
KD = D_MODEL // P
H_RET, DK, DV = 4, 128, 128
RET_W = H_RET * DV
H_SSD, P_SSD, G_SSD, N_SSD = 16, 64, 2, 64
SSD_W = H_SSD * P_SSD
HPG = H_SSD // G_SSD
CONV_K = 4
CONV_DIM = SSD_W + 2 * G_SSD * N_SSD
NCT = CONV_DIM // P
N_GRP, EXP_PG, N_EXP, D_FF = 4, 4, 16, 512
EPS = 1e-6
UNIT = 512
HALF = TOK // 2
HPRE = SEQ - HALF

COL_Q, COL_K, COL_V, COL_RG = 0, 512, 1024, 1536
COL_Z = 4 * RET_W
COL_X = COL_Z + SSD_W
COL_DT = COL_X + CONV_DIM
COL_GR = COL_DT + H_SSD
COL_GS = COL_GR + D_MODEL
IN_COLS = COL_GS + D_MODEL

CAP = P
MAIN = N_EXP
MAIN_CAP = CAP
OVER = TOK * 2 // (MAIN_CAP + 1)
TILES = MAIN + OVER
SLOTS = TILES * CAP
RING = 3
BIG = 1e30

UNITS = [("q", COL_Q, 512), ("k", COL_K, 512), ("v", COL_V, 512), ("rg", COL_RG, 512),
         ("x0", COL_X, 512), ("x1", COL_X + 512, 512), ("x2", COL_X + 1024, 256 + H_SSD),
         ("z0", COL_Z, 512), ("z1", COL_Z + 512, 512),
         ("ro", 0, 0), ("gr0", COL_GR, 512), ("gr1", COL_GR + 512, 512),
         ("so0", 0, 512), ("gs0", COL_GS, 512), ("so1", 512, 512), ("gs1", COL_GS + 512, 512),
         ("wo0", 0, 512), ("wo1", 512, 512)]
UNIT_NO = {u[0]: i for i, u in enumerate(UNITS)}
PHASE_USES = len(UNITS) // RING


def rows(t):
    return P if t < SAMPLE else NSAMP


def tok(t):
    return slice(P * t, P * t + rows(t))


def gammas():
    return 1.0 - 2.0 ** (-5.0 - np.arange(H_RET))


def constants():
    i = np.arange(P)
    g = gammas()
    scale = DK ** -0.5
    c = {"ident": np.eye(P), "upto": (i[:, None] <= i[None, :]), "before": (i[:, None] < i[None, :]), "ones": np.ones((P, P))}
    same = (i[:, None] // DEC_S == i[None, :] // DEC_S)
    up_s = (same & (i[:, None] <= i[None, :]))[:, :NSAMP]
    c["upto_s"] = up_s
    c["ones_s"] = same[:, :NSAMP]
    rel = (i[None, :] - i[:, None])
    c["decay"] = np.concatenate([np.where(rel >= 0, x ** np.maximum(rel, 0), 0) * scale for x in g], 1)
    c["decay_s"] = np.concatenate([np.where(up_s, x ** np.maximum(rel[:, :NSAMP], 0), 0) * scale for x in g], 1)
    c["kdec"] = scale * g[None, :] ** (P - 1 - i[:, None])
    c["kdec_s"] = scale * g[None, :] ** (DEC_S - 1 - i[:, None] % DEC_S)
    c["qdec"] = g[None, :] ** (i[:, None] + 1)
    c["qdec_s"] = g[None, :] ** (i[:, None] % DEC_S + 1)
    seq_of = np.arange(NSAMP) // DEC_S
    c["seqrow"] = np.tile((np.arange(DEC_B)[:, None] == seq_of[None, :]).reshape(1, -1), (P, 1))
    c["seqcol"] = (i[:, None] // DEC_S == np.arange(DEC_B)[None, :])
    half = DK // 2
    pos = np.concatenate([np.arange(SEQ), PAST + np.tile(np.arange(DEC_S), DEC_B)]).astype(np.float32)
    inv = np.power(np.float32(10000.0), -np.arange(half, dtype=np.float32) / np.float32(half))
    ang = (pos[None, :] * inv[:, None]).astype(np.float64)
    c["slot0"] = np.tile(CAP * np.arange(N_EXP)[None, :], (P, 1))
    c["back16"] = np.tile(np.arange(N_EXP)[None, :] - N_EXP, (P, 1))
    c["back4"] = np.tile(np.arange(N_GRP)[None, :] - N_GRP, (P, 1))
    c["expno"] = np.tile(np.arange(N_EXP)[None, :], (P, 1))
    c["overno"] = np.tile(np.arange(OVER)[None, :], (P, 1))
    c["valid"] = (i[:, None] + P * np.arange(NT)[None, :] < TOK)
    c["cos"] = np.concatenate([np.cos(ang), np.cos(ang)], 0)
    c["sin"] = np.concatenate([-np.sin(ang), np.sin(ang)], 0)
    return {k: np.asarray(v, np.float32) for k, v in c.items()}


CONST_AT = {}
_n = 0
for _k, _v in constants().items():
    CONST_AT[_k] = (_n, _v.shape[1])
    _n += _v.shape[1]
CONST_COLS = CONST_AT["cos"][0]


class Signal:

    def __init__(self, sem, name, plan):
        self.sem, self.name, self.plan, self.total, self.seen = sem, name, plan, 0, {}
        self.last = plan.get((name, "total"), 0)

    def mark(self, ins, key, n=1):
        self.total += n
        ins.then_inc(self.sem, n)
        self.plan[self.name, key] = self.total
        self.plan[self.name, "total"] = self.total

    def wait(self, eng, key, layer=None):
        value = self.plan.get((self.name, key), 1)
        if layer is not None:
            eng.wait_ge(self.sem, layer * self.last + value)
        elif self.seen.get(id(eng), 0) < value:
            self.seen[id(eng)] = value
            eng.wait_ge(self.sem, value)


class Bank:

    def __init__(self, ap, full, free, plan, no):
        self.ap, self.full, self.free, self.plan, self.no, self.order = ap, full, free, plan, no, []
        self.given, self.seen = {}, {}

    def acquire(self, pe, key):
        need = sum(self.plan.get(("released", self.no, k), 1) for k in self.order)
        if need:
            pe.wait_ge(self.free, need)
        self.order.append(key)
        self.plan["fill", self.no, key] = len(self.order)
        self.plan["all", self.no] = [k for k in self.order]

    def filled(self, ins):
        ins.then_inc(self.full, 1)

    def wait(self, eng, key):
        eng.wait_ge(self.full, self.plan.get(("fill", self.no, key), 1))

    def release(self, ins, key):
        self.given[key] = self.given.get(key, 0) + 1
        self.plan["released", self.no, key] = self.given[key]
        ins.then_inc(self.free, 1)

    def wait_freed(self, eng, key):
        order = self.plan.get(("all", self.no), [])
        upto = order[:order.index(key) + 1] if key in order else []
        need = sum(self.plan.get(("released", self.no, k), 1) for k in upto) or 1
        if self.seen.get(id(eng), 0) < need:
            self.seen[id(eng)] = need
            eng.wait_ge(self.free, need)

    def releases(self):
        return sum(self.plan.get(("released", self.no, k), 1) for k in self.plan.get(("all", self.no), []))


def build(nc, plan, x_p, x_s, state_ret, state_ssm, state_conv, ln1_g, w_in, ret_gn_g, w_ret_out, conv_w, conv_b,
          dt_bias, a_log, d_skip, ssd_norm_g, w_ssd_out, w_o, ln2_g, w_rg, w_re, w_gate, w_up, w_down, lnf_g,
          table, y_p, y_s, ret_p, ssm_p, conv_p, ret_s, ssm_s, conv_s):
    x_spill = nc.dram_tensor("x_spill", (NT * P, D_MODEL), F32, kind="Internal").ap()
    slot_in = nc.dram_tensor("slot_in", (SLOTS, D_MODEL), F32, kind="Internal").ap()
    slot_out = nc.dram_tensor("slot_out", (SLOTS, D_MODEL), F32, kind="Internal").ap()

    with ExitStack() as ctx:
        def sb(name, *free, dt=F32):
            return ctx.enter_context(nc.sbuf_tensor(name, [P, *free], dt))

        def sem(name):
            return ctx.enter_context(nc.semaphore(name))

        signals = {}

        def signal(name):
            if name not in signals:
                signals[name] = Signal(sem(name), name, plan)
            return signals[name]

        const = sb("const", CONST_COLS)
        ring = sb("ring", RING, 8 * UNIT)
        X = sb("X", NT, D_MODEL)
        ARENA = 31936
        arena = sb("arena", ARENA)
        small = sb("small", 1350)
        zero = sb("zero", 256)
        neg = sb("neg", P + NSAMP, dt=BF16)
        ident16 = sb("ident16", P, dt=BF16)
        slot_i = sb("slot_i", 2 * NT, dt=I32)
        over_i = sb("over_i", OVER + 1, dt=I32)

        def C(name, p=P):
            a, n = CONST_AT[name]
            return const[0:p, a:a + n]

        class Carve:
            def __init__(self, tensor, at, end):
                self.t, self.at, self.end = tensor, at, end

            def __call__(self, *free):
                n = int(np.prod(free))
                a = self.t[:, self.at:self.at + n]
                self.at += n
                assert self.at <= self.end, (self.at, self.end)
                if len(free) == 1:
                    return a
                names = " ".join("abcd"[:len(free)])
                return a.rearrange(f"p ({names}) -> p {names}", **{"abcd"[i]: free[i] for i in range(len(free))})

        S = Carve(small, 0, 1350)
        A = Carve(arena, 0, ARENA)
        hT = A(KD, TOK)
        qk = A(KD + 3, TOK)
        onT = A(RET_W // P, TOK)
        yT = A(KD, TOK)
        nat = A(DEC_B * 8, 64)
        tmp0 = A.at
        conv = qk
        mT = qk[:, 0:KD, :]
        yflat = yT.rearrange("p k n -> p (k n)")
        cvn_in, cvo_n, S_ret = yflat[:, 0:1280], yflat[:, 1280:2560], yflat[:, 2560:3072]
        vexp = yflat[:, 3072:4096].rearrange("p (b v) -> p b v", b=DEC_B)
        natS = nat.rearrange("p (b h g) k -> p b h g k", b=DEC_B, g=G_SSD)
        natR = nat.rearrange("p (b h x) k -> p b h (x k)", b=DEC_B, h=H_RET)
        ssmT = X[:, 0:4, :].rearrange("p a b -> p (a b)").rearrange("p (b c) -> p b c", b=DEC_B)

        g1, g2, conv_wT, conv_bT = S(KD), S(KD), S(NCT, CONV_K), S(NCT)
        gnT, sngT = S(RET_W // P), S(KD)
        dskip, alog, dtb, acoef = S(H_SSD), S(H_SSD), S(H_SSD), S(H_SSD)
        wr_g, wr_e = S(KD, N_GRP), S(KD, N_EXP)
        ssq, nvar, nln, nrs, nnt, nrms = (S(NT) for _ in range(6))
        ssq2, nvar2, nln2, nrs2, nnt2, nrms2 = (S(NT) for _ in range(6))
        dts, dt1, dt2, dt3, dta = (S(NT, H_SSD) for _ in range(5))
        cum, cend, ncum, ecum, wend, dec = (S(NT, H_SSD) for _ in range(6))
        gsum, gvar, gln, grs, gnt, grms = (S(4) for _ in range(6))
        ysum, yvar, yln, yrs, ynt, yrms = (S(2) for _ in range(6))
        E8 = S(8, DEC_B)
        mark_row = S(2)

        T = Carve(arena, tmp0, ARENA)
        hn = T(2, D_MODEL)
        sqj = T(2, D_MODEL)
        rope = T(2, TOK)
        xsw, rot1, rot2 = T(2, HALF), T(2, HALF), T(2, HALF)
        T = Carve(arena, tmp0, ARENA)
        vt, rgs, erg, ktok, sc = T(2, RET_W), T(2, RET_W), T(2, RET_W), T(2, RET_W), T(2, RET_W)
        ret_o, ret_c, ret_q = T(RET_W), T(RET_W), T(RET_W)
        qexp = T(H_RET, NSAMP * DEC_B)
        T = Carve(arena, tmp0, ARENA)
        S_ssm = T(8 * P_SSD)
        scv, cvo = T(NCT, 24), T(NCT, 27)
        xr = T(2, CONV_K - 1 + SEQ + DEC_B * (DEC_S + 3))
        cb_, ce = T(2, TOK), T(2, TOK)
        T = Carve(arena, tmp0 + 8 * P_SSD, ARENA)
        xs, xdt, wx, ud, wl = T(SSD_W), T(SSD_W), T(SSD_W), T(2, 4 * P), T(H_SSD * P)
        yb, ez, zs, btz = T(SSD_W), T(SSD_W), T(SSD_W), T(2, P)
        czexp = wl[:, 1024:2048]
        spo = zs[:, 0:512]
        yjunk, bexp = ez[:, 0:512], ez[:, 512:1024]
        dtx = ud.rearrange("p a b -> p (a b)")
        ge, mix2 = xs[:, 0:2 * HALF].rearrange("p (a b) -> p a b", a=2), xdt[:, 0:HALF]
        T = Carve(arena, tmp0, ARENA)
        glog, elog = T(NT, N_GRP), T(NT, N_EXP)
        rt1, rt2, rt3, rt4 = (T(NT) for _ in range(4))
        gmax, gden, gidx, m1, m2, i1, i2, w1, w2 = (T(NT) for _ in range(9))
        r4a, r4b = T(NT, N_GRP), T(NT, N_GRP)
        ra, rb, oh1, oh2, hit, rank, slot_e = (T(NT, N_EXP) for _ in range(7))
        tot, otile, obase, oscan, oend = (T(N_EXP) for _ in range(5))
        slots_f = T(2, NT)
        ov_a, ov_b, ov_c = T(OVER, N_EXP), T(OVER, N_EXP), T(OVER)
        T = Carve(arena, 0, tmp0)
        xn = T(NT, D_MODEL)
        tT = T(2, KD, P)
        xrow = T(2, D_MODEL)
        xsT = T(2, KD, P)
        fe, fa, aT, fo = T(D_FF), T(2, D_FF), T(2, 4, P), T(2, D_MODEL)
        sq2 = T(D_MODEL)
        gf = T(D_MODEL)
        T = Carve(arena, NT * D_MODEL, ARENA)
        got = T(2 * NT, D_MODEL)

        banks = []
        for i in range(8):
            ap = ctx.enter_context(nc.psum_tensor(f"psum{i}", [P, 512], F32))
            banks.append(Bank(ap[:, :], sem(f"psum{i}_full"), sem(f"psum{i}_free"), plan, i))
        bk = [b.ap for b in banks]

        slot_loaded = [sem(f"slot_loaded{i}") for i in range(RING)]
        slot_used = [sem(f"slot_used{i}") for i in range(RING)]
        engines_done, layer_cleared, aside = sem("engines_done"), sem("layer_cleared"), sem("aside")
        scattered = sem("scattered")
        gathered = [sem(f"gathered{i}") for i in range(2 * NT)]
        setup_loaded, setup_made, zeroed, final_loaded, final_made, stored = (
            sem(n) for n in ("setup_loaded", "setup_made", "zeroed", "final_loaded", "final_made", "stored"))
        for n in plan.get("names", ()):
            signal(n)
        xrow_in = [sem(f"xrow_in{s}") for s in range(2)]
        out_stored = [sem(f"out_stored{s}") for s in range(2)]
        x_T, x_Tc, gate_up, sig_e, acted, act_T, act_Tc, down_ok, out_ok = (
            sem(n) for n in ("rows_turned", "rows_copied", "gate_up_done", "expo_done", "acted", "act_turned", "act_copied",
                             "down_done", "out_copied"))
        moe_chain = sem("moe_chain")
        loop_sems = xrow_in + out_stored + [x_T, x_Tc, gate_up, sig_e, acted, act_T, act_Tc, down_ok, out_ok, moe_chain]

        block = ctx.enter_context(nc.Block())
        G = [float(v) for v in gammas()]

        def bc(ap, n):
            return ap.unsqueeze(len(ap.shape)).broadcast_to([*ap.shape, n])

        def bm(ap, n):
            return ap.unsqueeze(1).broadcast_to([ap.shape[0], n, *ap.shape[1:]])

        def ring_slot(name):
            n = UNIT_NO[name]
            return n % RING, n // RING

        def need_unit(pe, name):
            s, n = ring_slot(name)
            pe.wait_ge(slot_loaded[s], 16 * (n + 1))

        def unit_done(ins, name):
            ins.then_inc(slot_used[ring_slot(name)[0]], 1)

        def win(name):
            return ring[:, ring_slot(name)[0], :].rearrange("p (k n) -> p k n", k=KD)

        def meet(eng, L):
            eng.drain().then_inc(engines_done, 1)
            eng.wait_ge(layer_cleared, L + 1)
            eng.sem_inc(aside, 1)

        @block.sync
        def _(sp):
            sp.dma_start(const[:], table[:, 0:CONST_COLS]).then_inc(setup_loaded, 16)
            sp.dma_start(X[:, 0:4, :], x_p.rearrange("b (t p) d -> p (b t) d", p=P)).then_inc(setup_loaded, 16)
            sp.dma_start(X[0:NSAMP, SAMPLE, :], x_s.rearrange("b s d -> (b s) d")).then_inc(setup_loaded, 16)
            sp.wait_ge(setup_loaded, 48)
            with sp.Fori(0, DEPTH) as L:
                for s in range(RING):
                    sp.sem_inc(slot_used[s], 1)
                signal("rope").mark(sp.dma_start(rope.rearrange("p a t -> p (a t)"), table[:, CONST_COLS:]), "in", 16)
                cc = nc.allow_non_contiguous_dma(reason="small per-feature vectors")
                with cc:
                    for dst, src, key in (
                            (g1, ln1_g[L].rearrange("(k p) -> p k", p=P), "g1"),
                            (conv_bT, conv_b[L].rearrange("(k p) -> p k", p=P), "cb"),
                            (gnT, ret_gn_g[L].rearrange("(k p) -> p k", p=P), "gn"),
                            (sngT, ssd_norm_g[L].rearrange("(k p) -> p k", p=P), "sng"),
                            (g2, ln2_g[L].rearrange("(k p) -> p k", p=P), "g2")):
                        signal("g1" if key == "g1" else "vectors").mark(sp.dma_start(dst, src), "in", 16)
                    for j in range(CONV_K):
                        signal("vectors").mark(sp.dma_start(conv_wT[:, :, j], conv_w[L, j].rearrange("(k p) -> p k", p=P)), "in", 16)
                    for dst, src in ((dskip, d_skip), (alog, a_log), (dtb, dt_bias)):
                        signal("head_vectors").mark(sp.dma_start(dst, src[L].partition_broadcast(P)), "in", 16)
                    signal("router_w").mark(sp.dma_start(wr_g, w_rg[L].rearrange("(k p) n -> p k n", p=P)), "in", 16)
                    signal("router_w").mark(sp.dma_start(wr_e, w_re[L].rearrange("(k p) n -> p k n", p=P)), "in", 16)
                for b in range(0, DEC_B, 2):
                    signal("natR").mark(sp.dma_start(natR[:, b:b + 2], state_ret[L, b:b + 2].rearrange("b h k v -> k b h v")), "in", 16)

                sx = signal("x_spilled")
                sx.mark(sp.dma_start(x_spill[0:SEQ, :].rearrange("(t p) d -> p t d", p=P), X[:, 0:4, :]), "out", 16)

                def unit(name):
                    s, n = ring_slot(name)
                    sp.wait_ge(slot_used[s], n + 1)
                    _, col, w = UNITS[UNIT_NO[name]]
                    dst = ring[:, s, :]
                    if name == "ro":
                        src = w_ret_out[L].rearrange("(k p) n -> p k n", p=P)
                        dst = dst.rearrange("p (k n) -> p k n", k=RET_W // P)
                    elif name[0:2] in ("so", "wo"):
                        m = w_ssd_out if name[0] == "s" else w_o
                        src = m[L, :, col:col + w].rearrange("(k p) n -> p k n", p=P)
                        dst = dst.rearrange("p (k n) -> p k n", k=KD)
                    else:
                        src = w_in[L, :, col:col + w].rearrange("(k p) n -> p k n", p=P)
                        dst = dst.rearrange("p (k n) -> p k n", k=KD)[:, :, 0:w]
                    sp.dma_start(dst, src).then_inc(slot_loaded[s], 16)

                for name in ("q", "k", "v", "rg"):
                    unit(name)
                signal("scv_nat").mark(sp.dma_start(cvn_in[0:24, :], state_conv[L].rearrange("b j c -> (b j) c")), "in", 16)
                for name in ("x0", "x1", "x2"):
                    unit(name)
                banks[7].wait_freed(sp, ("kv", 3))
                signal("out_retp").mark(sp.dma_start(ret_p[L, 0].rearrange("h k v -> k h v"), S_ret.rearrange("p (h v) -> p h v", h=H_RET)), "out", 16)
                banks[7].wait_freed(sp, ("kvs", H_RET - 1, 0))
                banks[4].wait_freed(sp, ("kvs", H_RET - 1, 1))
                signal("out_rets").mark(sp.dma_start(ret_s[L].rearrange("b h k v -> k (b h) v"), nat.rearrange("p (c x) k -> p c (x k)", x=2)), "out", 16)
                signal("out_rets").wait(sp, "out")
                for c in range(8):
                    signal("natS").mark(sp.dma_start(natS[:, :, c % 4, c // 4, :], state_ssm[L, :, 2 * c:2 * c + 2].rearrange("b j p k -> (j p) b k")), "in", 16)
                unit("z0")
                unit("z1")
                for q in range(3):
                    banks[4 + q].wait_freed(sp, ("cvo", q))
                signal("out_convp").mark(sp.dma_start(conv_p[L, 0], cvo_n[0:3, :]), "out", 16)
                signal("out_convs").mark(sp.dma_start(conv_s[L].rearrange("b j c -> (b j) c"), cvo_n[3:27, :]), "out", 16)
                unit("ro")
                banks[4].wait_freed(sp, ("spo",))
                for g in range(G_SSD):
                    signal("out_ssmp").mark(sp.dma_start(ssm_p[L, 0, 8 * g:8 * g + 8].rearrange("(c j) p k -> (j p) c k", j=2),
                                                         spo.rearrange("p (c g k) -> p c g k", g=2, k=64)[:, :, g, :]), "out", 16)
                unit("gr0")
                unit("gr1")
                banks[4].wait_freed(sp, ("bxs", 7))
                for c in range(8):
                    signal("out_ssms").mark(sp.dma_start(ssm_s[L, :, 2 * c:2 * c + 2].rearrange("b j p k -> (j p) b k"), natS[:, :, c % 4, c // 4, :]), "out", 16)
                sx.wait(sp, "out")
                banks[6].wait(sp, ("yst", SAMPLE, 1))
                sx.mark(sp.dma_start(X[:, 0:4, :], x_spill[0:SEQ, :].rearrange("(t p) d -> p t d", p=P)), "in", 16)
                for name in ("so0", "gs0", "so1", "gs1", "wo0", "wo1"):
                    unit(name)

                def load_rows(j, s, after):
                    if after is not None:
                        sp.wait_ge(x_T, after)
                    sp.dma_start(xrow[:, s, :], slot_in[bass.ds(j * P, P), :]).then_inc(xrow_in[s], 16)

                def load_expert(which, e_no, use):
                    sp.wait_ge(slot_used[which], use)
                    m = (w_gate, w_up, w_down)[which]
                    sp.dma_start(ring[:, which, :].rearrange("p (k n) -> p k n", k=(KD, KD, D_FF // P)[which]),
                                 m[L, e_no].rearrange("(k p) n -> p k n", p=P)).then_inc(slot_loaded[which], 16)

                for key in ("retp", "rets", "convp", "convs", "ssmp", "ssms"):
                    signal("out_" + key).wait(sp, "out")

                def load_tiles(first, count, expert):
                    def pair(j, e):
                        load_expert(0, e, j + (PHASE_USES + 1))
                        load_expert(1, e, j + (PHASE_USES + 1))

                    pair(first, expert(first))
                    signal("rows_ready").wait(sp, "all")
                    load_rows(first, 0, first - 1 if first else None)
                    load_rows(first + 1, 1, first if first else None)
                    if first == 0:
                        with sp.Fori(0, (count - 2) // 2) as t2:
                            for s in range(2):
                                j = t2 * 2 + (first + s)
                                pair(j + 1, j + 1)
                                load_rows(j + 2, s, j + 1)
                                load_expert(2, j, j + (PHASE_USES + 1))
                        peeled = range(first + count - 2, first + count)
                    else:
                        peeled = range(first, first + count)
                    for j in peeled:
                        if j + 1 < first + count:
                            pair(j + 1, expert(j + 1))
                        if j + 2 < first + count:
                            load_rows(j + 2, j % 2, j + 1)
                        load_expert(2, expert(j), j + (PHASE_USES + 1))

                load_tiles(0, MAIN, lambda j: j)
                n_extra = sp.value_load(over_i[0:1, OVER:OVER + 1], min_val=0, max_val=OVER)
                with sp.If(n_extra > 0):
                    e_of = {}

                    def named(j):
                        if j not in e_of:
                            e_of[j] = sp.value_load(over_i[0:1, j - MAIN:j - MAIN + 1], min_val=0, max_val=N_EXP - 1)
                        return e_of[j]

                    load_tiles(MAIN, OVER, named)

                sp.wait_ge(engines_done, L * 4 + 4)
                sp.sem_inc(aside, 1)
                for s in [x.sem for x in signals.values()] + [b.full for b in banks] + [b.free for b in banks] + loop_sems + slot_loaded + slot_used:
                    sp.sem_clear(s)
                sp.sem_inc(layer_cleared, 1)
            sp.dma_start(gf, lnf_g.partition_broadcast(P)).then_inc(final_loaded, 16)
            sp.wait_ge(final_made, 1)
            sp.dma_start(y_p.rearrange("b (t p) d -> p (b t) d", p=P), xn[:, 0:4, :]).then_inc(stored, 16)
            sp.dma_start(y_s.rearrange("b s d -> (b s) d"), xn[0:NSAMP, SAMPLE, :]).then_inc(stored, 16)
            sp.wait_ge(stored, 32)

        @block.tensor
        def _(pe):
            W = nc.tensor
            pe.wait_ge(setup_loaded, 48)
            pe.wait_ge(setup_made, 1)

            def turn(bank, key, srcs, wait=None, width=P):
                b = banks[bank]
                b.acquire(pe, key)
                if wait:
                    signal(wait[0]).wait(pe, wait[1])
                for i, src in enumerate(srcs):
                    n, m = src.shape[0], int(np.prod(src.shape[1:]))
                    last = W.transpose(b.ap[0:m, i * width:i * width + n], src, C("ident", n)[:, 0:n])
                b.filled(last)

            def fmajor(name, cc, half, bank, key, lhs_k=KD, rhs=None, last_of=False):
                rhs = hT if rhs is None else rhs
                w = ring[:, ring_slot(name)[0], :].rearrange("p (k n) -> p k n", k=lhs_k)
                b = banks[bank]
                b.acquire(pe, key)
                for k in range(lhs_k):
                    last = W.matmul(b.ap[:, 0:HALF], w[:, k, cc * P:cc * P + P], rhs[:, k, half * HALF:(half + 1) * HALF],
                                    start=(k == 0), stop=(k == lhs_k - 1))
                b.filled(last)
                return last

            def tmajor(name, t, bank, key, src=None):
                src = hT if src is None else src
                b = banks[bank]
                b.acquire(pe, key)
                for k in range(KD):
                    last = W.matmul(b.ap[0:rows(t), :], src[:, k, tok(t)], win(name)[:, k, :], start=(k == 0), stop=(k == KD - 1))
                b.filled(last)

            def done(name):
                W.drain().then_inc(slot_used[ring_slot(name)[0]], 1)

            with pe.Fori(0, DEPTH) as L:
                for t in range(NT):
                    for h in range(2):
                        turn(2 + h, ("hT", t, h), [hn[0:rows(t), t % 2, (4 * h + i) * P:(4 * h + i + 1) * P] for i in range(4)],
                             ("hn", t))
                g = 0
                for u, name in enumerate(("q", "k")):
                    need_unit(pe, name)
                    for cc in range(4):
                        for half in range(2):
                            for h in range(2):
                                banks[2 + h].wait_freed(pe, ("hT", NT - 1 if half else 2, h))
                            fmajor(name, cc, half, g % 2, ("qk", g))
                            g += 1
                    done(name)
                need_unit(pe, "v")
                need_unit(pe, "rg")
                for t in range(NT):
                    n = rows(t)
                    turn(2, ("ktok", t), [qk[:, 4 + h, tok(t)] for h in range(H_RET)], ("qk", 15 if t >= 2 else 14))
                    b = banks[4]
                    b.acquire(pe, ("scores", t))
                    for h in range(H_RET):
                        last = W.matmul(b.ap[0:n, h * n:(h + 1) * n], qk[:, 4 + h, tok(t)], qk[:, h, tok(t)], start=True, stop=True)
                    b.filled(last)
                    tmajor("v", t, 0, ("v", t))
                    tmajor("rg", t, 1, ("rg", t))
                    if t == SAMPLE:
                        done("v")
                        done("rg")
                    banks[4].wait_freed(pe, ("scores", t))
                    banks[0].wait_freed(pe, ("v", t))
                    b = banks[5]
                    b.acquire(pe, ("intra", t))
                    for h in range(H_RET):
                        last = W.matmul(b.ap[0:n, h * DV:(h + 1) * DV], sc[0:n, t % 2, h * n:(h + 1) * n],
                                        vt[0:n, t % 2, h * DV:(h + 1) * DV], start=True, stop=True)
                    b.filled(last)
                    b = banks[6]
                    b.acquire(pe, ("inter", t))
                    if t < SAMPLE:
                        signal("state_zero").wait(pe, "ret")
                        if t:
                            banks[7].wait_freed(pe, ("kv", t - 1))
                        for h in range(H_RET):
                            last = W.matmul(b.ap[:, h * DV:(h + 1) * DV], qk[:, h, tok(t)], S_ret[:, h * DV:(h + 1) * DV], start=True, stop=True)
                    else:
                        signal("natR").wait(pe, "in")
                        for h in range(H_RET):
                            signal("qexp").wait(pe, h)
                            for q in range(DEC_B):
                                last = W.matmul(b.ap[0:n, h * DV:(h + 1) * DV], qexp[:, h, q * NSAMP:(q + 1) * NSAMP], natR[:, q, h, :],
                                                start=(q == 0), stop=(q == DEC_B - 1))
                    b.filled(last)
                    banks[2].wait_freed(pe, ("ktok", t))
                    if t < SAMPLE:
                        b = banks[7]
                        b.acquire(pe, ("kv", t))
                        for h in range(H_RET):
                            last = W.matmul(b.ap[:, h * DV:(h + 1) * DV], ktok[:, t % 2, h * DV:(h + 1) * DV], vt[:, t % 2, h * DV:(h + 1) * DV],
                                            start=True, stop=True)
                        b.filled(last)
                    else:
                        for h in range(H_RET):
                            signal("vexp").wait(pe, h)
                            for q in range(2):
                                b = banks[(7, 4)[q]]
                                b.acquire(pe, ("kvs", h, q))
                                last = W.matmul(b.ap[:, :], ktok[0:n, t % 2, h * DV:(h + 1) * DV],
                                                vexp[0:n, 4 * q:4 * q + 4, :].rearrange("p b v -> p (b v)"), start=True, stop=True)
                                b.filled(last)
                    if t >= 1:
                        turn(3, ("onT", t - 1), [ret_q[0:rows(t - 1), i * P:(i + 1) * P] for i in range(4)], ("gated", t - 1))
                turn(3, ("onT", SAMPLE), [ret_q[0:NSAMP, i * P:(i + 1) * P] for i in range(4)], ("gated", SAMPLE))
                turn(2, ("scv",), [cvn_in[0:24, i * P:(i + 1) * P] for i in range(NCT)], ("scv_nat", "in"), width=24)
                g = 0
                for name, n_cc in (("x0", 4), ("x1", 4), ("x2", 2)):
                    need_unit(pe, name)
                    for cc in range(n_cc):
                        for half in range(2):
                            fmajor(name, cc, half, half, ("x", g, half))
                        g += 1
                    if name != "x2":
                        done(name)
                b = banks[3]
                b.acquire(pe, ("dt",))
                for t in range(NT):
                    for k in range(KD):
                        last = W.matmul(b.ap[0:rows(t), t * H_SSD:(t + 1) * H_SSD], hT[:, k, tok(t)], win("x2")[:, k, 256:256 + H_SSD],
                                        start=(k == 0), stop=(k == KD - 1))
                b.filled(last)
                done("x2")
                for q, (a, z) in enumerate(((0, 4), (4, 8), (8, 10))):
                    turn(4 + q, ("cvo", q), [cvo[:, i, :] for i in range(a, z)], ("cvo", NCT - 1))
                need_unit(pe, "z0")
                need_unit(pe, "z1")
                b = banks[3]
                b.acquire(pe, ("cum",))
                signal("dta").wait(pe, 0)
                for t in range(NT):
                    n = rows(t)
                    for q, m in enumerate((("upto", "ones") if t < SAMPLE else ("upto_s", "ones_s"))):
                        last = W.matmul(b.ap[0:n, t * 32 + 16 * q:t * 32 + 16 * q + 16], C(m, n)[:, 0:n], dta[0:n, t, :], start=True, stop=True)
                b.filled(last)
                for t in range(NT):
                    n = rows(t)
                    if t == SAMPLE:
                        for r in range(8):
                            turn(2 + r % 2, ("ssmT", r), [natS[:, r, h, :, :].rearrange("p g k -> p (g k)") for h in range(4)],
                                 ("natS", "in"))
                    for h in range(2):
                        if t == 0:
                            signal("conv").wait(pe, NCT - 1)
                        turn(2 + h, ("xsT", t, h), [conv[:, 4 * h + i, tok(t)] for i in range(4)])
                    b = banks[4]
                    b.acquire(pe, ("cb", t))
                    W.matmul(b.ap[0:n, 0:2 * n], conv[:, 8, tok(t)], conv[:, 9:11, tok(t)], start=True, stop=True)
                    b.filled(W.transpose(b.ap[0:n, 256:384], conv[:, 8, tok(t)], C("ident")))
                    tmajor("z0", t, 0, ("z", t, 0))
                    tmajor("z1", t, 1, ("z", t, 1))
                    if t == SAMPLE:
                        done("z0")
                        done("z1")
                    for r in range(4):
                        b = banks[5 + r % 2]
                        b.acquire(pe, ("seg", t, r))
                        mask = neg[0:n, 0:P] if t < SAMPLE else neg[0:n, P:P + NSAMP]
                        for h in range(4):
                            W.matmul(b.ap[0:n, h * n:(h + 1) * n], ident16[0:n, 0:n], mask, start=(h == 0), stop=False, skip_group_check=True)
                        signal("ud").wait(pe, (t, r))
                        last = W.matmul(b.ap[0:n, 0:4 * n], C("ones", n)[:, 0:n], ud[0:n, r % 2, 0:4 * n], start=False, stop=True, skip_group_check=True)
                        b.filled(last)
                    banks[4].wait_freed(pe, ("cb", t))
                    for h in range(2):
                        banks[2 + h].wait_freed(pe, ("xsT", t, h))
                    for g in range(2):
                        b = banks[2 + g]
                        b.acquire(pe, ("yin", t, g))
                        for h in range(8):
                            hh = 8 * g + h
                            last = W.matmul(b.ap[0:n, h * 64:(h + 1) * 64], wl[0:n, hh * n:(hh + 1) * n], xdt[0:n, hh * 64:(hh + 1) * 64], start=True, stop=True)
                        b.filled(last)
                    if t < SAMPLE:
                        signal("state_zero").wait(pe, "ssm")
                        if t:
                            banks[7].wait_freed(pe, ("bx", t - 1))
                    for g in range(2):
                        b = banks[5 + g]
                        b.acquire(pe, ("yst", t, g))
                        if t < SAMPLE:
                            last = W.matmul(b.ap[:, :], conv[:, 9 + g, tok(t)], S_ssm, start=True, stop=True)
                        else:
                            for r in (6, 7):
                                banks[2 + r % 2].wait_freed(pe, ("ssmT", r))
                            signal("czexp").wait(pe, g)
                            for q in range(DEC_B):
                                last = W.matmul(b.ap[0:n, :], czexp[:, g * 512 + q * 64:g * 512 + (q + 1) * 64], ssmT[:, q, :], start=(q == 0), stop=(q == DEC_B - 1))
                        b.filled(last)
                    signal("btz").wait(pe, t)
                    signal("wx").wait(pe, t)
                    if t < SAMPLE:
                        b = banks[7]
                        b.acquire(pe, ("bx", t))
                        for g in range(2):
                            last = W.matmul(b.ap[:, :], btz[:, g, :], wx[:, g * 512:(g + 1) * 512], start=(g == 0), stop=(g == 1))
                        b.filled(last)
                    else:
                        b = banks[7]
                        b.acquire(pe, ("e8",))
                        signal("dtx").wait(pe, 0)
                        for c in range(8):
                            last = W.matmul(b.ap[:, c * 8:(c + 1) * 8], dtx[0:n, c * P:(c + 1) * P], C("seqcol", n), start=True, stop=True)
                        b.filled(last)
                        for c in range(8):
                            b = banks[(7, 4)[c % 2]]
                            b.acquire(pe, ("bxs", c))
                            signal("bexp").wait(pe, c // 4)
                            last = W.matmul(b.ap[:, :], wx[0:n, c * P:(c + 1) * P], bexp[0:n, :], start=True, stop=True)
                            b.filled(last)
                    if t >= 1:
                        for h in range(2):
                            turn(h, ("yT", t - 1, h), [yb[0:rows(t - 1), (4 * h + i) * P:(4 * h + i + 1) * P] for i in range(4)], ("y", t - 1))
                    if t == SAMPLE - 1:
                        banks[7].wait_freed(pe, ("bx", t))
                        turn(4, ("spo",), [S_ssm[:, i * P:(i + 1) * P] for i in range(4)])
                for h in range(2):
                    turn(h, ("yT", SAMPLE, h), [yb[0:NSAMP, (4 * h + i) * P:(4 * h + i + 1) * P] for i in range(4)], ("y", SAMPLE))
                g = 0
                for br, out_names, gate_names, src, kk in ((0, ("ro", "ro"), ("gr0", "gr1"), onT, 4), (1, ("so0", "so1"), ("gs0", "gs1"), yT, KD)):
                    for c in range(KD):
                        un, gn = out_names[c // 4], gate_names[c // 4]
                        if c % 4 == 0:
                            need_unit(pe, gn)
                            if br or c == 0:
                                need_unit(pe, un)
                        for half in range(2):
                            fmajor(gn, c % 4, half, g % 2, ("gate", g))
                            if br == 0:
                                banks[3].wait_freed(pe, ("onT", SAMPLE))
                            else:
                                for h in range(2):
                                    banks[h].wait_freed(pe, ("yT", SAMPLE, h))
                            fmajor(un, c if br == 0 else c % 4, half, 2 + g % 2, ("branch", g), lhs_k=kk, rhs=src)
                            g += 1
                        if c % 4 == 3:
                            if br or c == 7:
                                done(un)
                            done(gn)
                need_unit(pe, "wo0")
                need_unit(pe, "wo1")
                signal("mix").wait(pe, 31)
                for t in range(NT):
                    for h in range(2):
                        tmajor(f"wo{h}", t, 4 + (2 * t + h) % 4, ("wo", t, h), src=mT)
                done("wo0")
                done("wo1")
                signal("router_w").wait(pe, "in")
                rbank = banks[0]
                rbank.acquire(pe, ("router",))
                for t in range(NT):
                    for h in range(2):
                        turn(2 + h, ("tT", t, h), [xn[0:rows(t), t, (4 * h + i) * P:(4 * h + i + 1) * P] for i in range(4)], ("xn", t))
                    for h in range(2):
                        banks[2 + h].wait_freed(pe, ("tT", t, h))
                    for w, n, a in ((wr_g, N_GRP, 0), (wr_e, N_EXP, N_GRP)):
                        for k in range(KD):
                            last = W.matmul(rbank.ap[0:rows(t), t * 20 + a:t * 20 + a + n], tT[:, t % 2, k, 0:rows(t)], w[:, k, :],
                                            start=(k == 0), stop=(k == KD - 1))
                    if t < SAMPLE:
                        signal("routed").mark(last, t)
                rbank.filled(last)
                signal("hit").wait(pe, 0)
                b = banks[1]
                b.acquire(pe, ("rank",))
                for t in range(NT):
                    for q in range(t + 1):
                        n = rows(t)
                        W.matmul(b.ap[0:n, t * 16:(t + 1) * 16], C("before", rows(q))[:, 0:n] if q == t else C("ones")[:, 0:n],
                                 hit[0:rows(q), q, :], start=(q == 0), stop=(q == t))
                for q in range(NT):
                    last = W.matmul(b.ap[:, 80:96], C("ones", rows(q)), hit[0:rows(q), q, :], start=(q == 0), stop=(q == NT - 1))
                b.filled(last)

                for b in banks:
                    if b.releases():
                        pe.wait_ge(b.free, b.releases())

                def weights(which, j_use):
                    pe.wait_ge(slot_loaded[which], j_use)

                def turn_rows(s, j, half_j):
                    pe.wait_ge(xrow_in[s], half_j * 16 + 16)
                    if not isinstance(j, int) or j > 1:
                        pe.wait_ge(act_Tc, j - 1)
                    elif j == 1:
                        pe.wait_ge(x_Tc, 1)
                    for i in range(KD):
                        last = W.transpose(bk[2 + i // 4][:, (i % 4) * P:(i % 4 + 1) * P], xrow[:, s, i * P:(i + 1) * P], C("ident"))
                    last.then_inc(x_T, 1)

                def gate_up_mm(s, j):
                    pe.wait_ge(x_Tc, j + 1)
                    if not isinstance(j, int) or j > 0:
                        pe.wait_ge(acted, j)
                    for which in range(2):
                        weights(which, j * 16 + 16 * (PHASE_USES + 1))
                        w = ring[:, which, :].rearrange("p (k n) -> p k n", k=KD)
                        for k in range(KD):
                            last = W.matmul(bk[which], xsT[:, s, k, :], w[:, k, :], start=(k == 0), stop=(k == KD - 1))
                        if which == 0:
                            last.then_inc(slot_used[0], 1)
                    last.then_inc(gate_up, 1)
                    W.drain().then_inc(slot_used[1], 1)

                def down_mm(s, j):
                    pe.wait_ge(act_Tc, j + 1)
                    pe.wait_ge(out_ok, j + 1)
                    weights(2, j * 16 + 16 * (PHASE_USES + 1))
                    w = ring[:, 2, :].rearrange("p (k n) -> p k n", k=4)
                    for h in range(2):
                        for k in range(4):
                            last = W.matmul(bk[4 + 2 * s + h], aT[:, s, k, :], w[:, k, h * 512:(h + 1) * 512], start=(k == 0), stop=(k == 3))
                    last.then_inc(down_ok, 1)
                    W.drain().then_inc(slot_used[2], 1)

                def turn_act(s, j, more=True):
                    pe.wait_ge(acted, j + 1)
                    if more:
                        pe.wait_ge(x_Tc, j + 2)
                    for i in range(4):
                        last = W.transpose(bk[2][:, i * P:(i + 1) * P], fa[:, s, i * P:(i + 1) * P], C("ident"))
                    last.then_inc(act_T, 1)

                def multiply_tiles(first, count):
                    last = first + count - 1
                    turn_rows(0, first, first // 2)
                    gate_up_mm(0, first)
                    turn_rows(1, first + 1, first // 2)
                    turn_act(0, first)
                    with pe.Fori(0, (count - 2) // 2) as t2:
                        for q in range(2):
                            s, j = 1 - q, t2 * 2 + (first + 1 + q)
                            gate_up_mm(s, j)
                            turn_rows(1 - s, j + 1, t2 + (first // 2 + 1))
                            down_mm(1 - s, j - 1)
                            turn_act(s, j)
                    gate_up_mm(1, last)
                    down_mm(0, last - 1)
                    turn_act(1, last, more=False)
                    down_mm(1, last)

                multiply_tiles(0, MAIN)
                signal("slots").wait(pe, "over")
                with pe.If(pe.value_load(over_i[0:1, OVER:OVER + 1], min_val=0, max_val=OVER) > 0):
                    multiply_tiles(MAIN, OVER)
                meet(pe, L)

        class Chain:

            def __init__(self, eng, name):
                self.eng, self.sig, self.n = eng, signal(name), 0

            def __call__(self, ins):
                self.n += 1
                self.sig.mark(ins, self.n)
                self.sig.wait(self.eng, self.n)

        @block.scalar
        def _(act):
            a = nc.scalar
            act.wait_ge(setup_loaded, 48)
            act.wait_ge(setup_made, 1)

            with act.Fori(0, DEPTH) as L:
                step = Chain(act, "act_step")

                def rsq(key, p, v, ln, rs):
                    signal("var").wait(act, key)
                    step(a.activation(ln[0:p], v[0:p], ACT.Ln))
                    signal("rs0").mark(a.activation(rs[0:p], ln[0:p], ACT.Exp, scale=-0.5), key)

                for t in range(NT):
                    if t >= 2:
                        signal("sq").wait(act, t - 2)
                    signal("sq").mark(a.activation(sqj[0:rows(t), t % 2, :], X[0:rows(t), t, :], ACT.Square, accum_out=ssq[0:rows(t), t:t + 1]), t)
                rsq("n1", P, nvar, nln, nrs)
                for g in range(16):
                    banks[g % 2].wait(act, ("qk", g))
                    if g >= 2:
                        banks[g % 2].wait_freed(act, ("qk", g - 2))
                    a.copy(xsw[0:64, g % 2, :], bk[g % 2][64:128, 0:HALF])
                    signal("xsw").mark(a.copy(xsw[64:128, g % 2, :], bk[g % 2][0:64, 0:HALF]), g)
                signal("qk").wait(act, 15)
                for t in range(NT):
                    n = rows(t)
                    banks[0].wait(act, ("v", t))
                    if t >= 2:
                        banks[5].wait(act, ("intra", t - 2))
                        banks[7].wait(act, ("kv", t - 2))
                    banks[0].release(a.copy(vt[0:n, t % 2, :], bk[0][0:n, :]), ("v", t))
                    banks[1].wait(act, ("rg", t))
                    if t >= 2:
                        banks[1].wait_freed(act, ("rg", t - 2))
                    signal("erg").mark(a.activation(erg[0:n, t % 2, :], bk[1][0:n, :], ACT.Exp, scale=-1.0), t)
                    rsq(("gn", t), n, gvar, gln, grs)
                signal("gated").wait(act, SAMPLE)
                banks[2].wait(act, ("scv",))
                banks[2].release(a.copy(scv.rearrange("p c r -> p (c r)"), bk[2][:, 0:24 * NCT]), ("scv",))
                banks[2].wait_freed(act, ("scv",))
                for g in range(NCT + 1):
                    if g < NCT:
                        pad = xr[:, g % 2, CONV_K - 1 + SEQ:].rearrange("p (b r) -> p b r", b=DEC_B)
                        if g >= 2:
                            signal("lin").wait(act, g - 2)
                            signal("cvo").wait(act, g - 2)
                        a.copy(pad[:, :, 0:3], scv[:, g, :].rearrange("p (b r) -> p b r", b=DEC_B))
                        banks[0].wait(act, ("x", g, 0))
                        banks[0].release(a.copy(xr[:, g % 2, 3:3 + HALF], bk[0][:, 0:HALF]), ("x", g, 0))
                        banks[1].wait(act, ("x", g, 1))
                        a.copy(xr[:, g % 2, 3 + HALF:3 + SEQ], bk[1][:, 0:HPRE])
                        banks[1].release(a.copy(pad[:, :, 3:], bk[1][:, HPRE:HALF].rearrange("p (b r) -> p b r", b=DEC_B)), ("x", g, 1))
                    if g >= 1:
                        signal("lin").wait(act, g - 1)
                        if g >= 3:
                            signal("conv").wait(act, g - 3)
                        signal("ce").mark(a.activation(ce[:, (g - 1) % 2, :], cb_[:, (g - 1) % 2, :], ACT.Exp, scale=-1.0), g - 1)
                signal("head_vectors").wait(act, "in")
                signal("acoef").mark(a.activation(acoef, alog, ACT.Exp), 0)
                signal("sp").wait(act, "arg")
                signal("spa").mark(a.activation(dt2, dt1, ACT.Exp), "e")
                signal("sp").wait(act, "u")
                signal("spa").mark(a.activation(dt3, dt1, ACT.Ln), "ln")
                for q in range(3):
                    w = (CONV_DIM - 512 * q) if q == 2 else 512
                    banks[4 + q].wait(act, ("cvo", q))
                    banks[4 + q].release(a.copy(cvo_n[0:27, 512 * q:512 * q + w], bk[4 + q][0:27, 0:w]), ("cvo", q))
                signal("decays").wait(act, "args")
                a.activation(ecum, cum, ACT.Exp)
                a.activation(dec, cend, ACT.Exp)
                signal("decayed").mark(a.activation(wend, wend, ACT.Exp), 0)
                signal("conv").wait(act, NCT - 1)
                for t in range(NT):
                    n = rows(t)
                    if t == SAMPLE:
                        signal("x_spilled").wait(act, "out")
                        for r in range(8):
                            b = banks[2 + r % 2]
                            b.wait(act, ("ssmT", r))
                            b.release(a.copy(ssmT[:, r, :], b.ap), ("ssmT", r))
                    for h in range(2):
                        b = banks[2 + h]
                        b.wait(act, ("xsT", t, h))
                        if t:
                            signal("ylin").wait(act, t - 1)
                        signal("xs").mark(a.copy(xs[0:n, 512 * h:512 * h + 512], b.ap[0:n, :]), (t, h))
                    if t:
                        banks[3].wait(act, ("yin", t - 1, 1))

                    def segs(r):
                        b = banks[5 + r % 2]
                        b.wait(act, ("seg", t, r))
                        for h in range(4):
                            hh = 4 * r + h
                            last = a.activation(wl[0:n, hh * n:(hh + 1) * n], b.ap[0:n, h * n:(h + 1) * n], ACT.Exp, bias=ncum[0:n, t, hh:hh + 1])
                        b.release(last, ("seg", t, r))

                    for h in range(2):
                        banks[h].wait(act, ("z", t, h))
                        if t:
                            banks[h].wait_freed(act, ("z", t - 1, h))
                        signal("ez").mark(a.activation(ez[0:n, 512 * h:512 * h + 512], bk[h][0:n, :], ACT.Exp, scale=-1.0), (t, h))
                    for r in range(4):
                        segs(r)
                    if t == SAMPLE:
                        banks[7].wait(act, ("e8",))
                        banks[7].release(a.activation(E8.rearrange("p c b -> p (c b)"), bk[7][:, 0:64], ACT.Exp), ("e8",))
                    signal("yz").wait(act, t)
                    if t == SAMPLE - 1:
                        banks[4].wait(act, ("spo",))
                        banks[4].release(a.copy(spo, bk[4]), ("spo",))
                    for g in range(2):
                        if g:
                            step(last)
                        last = a.activation(yjunk[0:n], yb[0:n, 512 * g:512 * g + 512], ACT.Square, accum_out=ysum[0:n, g:g + 1])
                    signal("ysq").mark(last, t)
                    rsq(("y", t), n, yvar, yln, yrs)
                signal("y").wait(act, SAMPLE)
                for g in range(32):
                    banks[g % 2].wait(act, ("gate", g))
                    if g >= 2:
                        banks[2 + g % 2].wait_freed(act, ("branch", g - 2))
                    banks[g % 2].release(a.activation(ge[:, g % 2, :], bk[g % 2][:, 0:HALF], ACT.Exp, scale=-1.0), ("gate", g))
                for t in range(NT):
                    for h in range(2):
                        banks[4 + (2 * t + h) % 4].wait_freed(act, ("wo", t, h))
                    if t:
                        signal("sq2").wait(act, t - 1)
                    signal("sq2").mark(a.activation(sq2[0:rows(t)], X[0:rows(t), t, :], ACT.Square, accum_out=ssq2[0:rows(t), t:t + 1]), t)
                rsq("n2", P, nvar2, nln2, nrs2)
                signal("route").wait(act, "gd")
                signal("routea").mark(a.activation(r4b, r4a, ACT.Exp), "g")
                signal("route").wait(act, "ed")
                signal("routea").mark(a.activation(rt2, rt1, ACT.Exp), "e")
                act.sem_inc(out_ok, 2)
                for s in range(2):
                    act.sem_inc(out_stored[s], 16)

                def expo(j):
                    act.wait_ge(gate_up, j + 1)
                    if not isinstance(j, int) or j:
                        act.wait_ge(acted, j)
                    a.activation(fe, bk[0], ACT.Exp, scale=-1.0).then_inc(sig_e, 1)

                def copy_act(s, j):
                    act.wait_ge(act_T, j + 1)
                    if not isinstance(j, int) or j > 1:
                        act.wait_ge(down_ok, j - 1)
                    a.copy(aT[:, s, :, :].rearrange("p k n -> p (k n)"), bk[2]).then_inc(act_Tc, 1)

                def store(s, j, nth):
                    act.wait_ge(down_ok, j + 1)
                    act.wait_ge(out_stored[s], nth * 16 + 16)
                    for h in range(2):
                        last = a.copy(fo[:, s, h * 512:(h + 1) * 512], bk[4 + 2 * s + h])
                    last.then_inc(out_ok, 1)
                    act.wait_ge(out_ok, j + 3)
                    act.dma_start(slot_out[bass.ds(j * P, P), :], fo[:, s, :]).then_inc(out_stored[s], 16)

                def finish_tiles(first, count):
                    last = first + count - 1
                    expo(first)
                    copy_act(0, first)
                    with act.Fori(0, (count - 2) // 2) as t2:
                        for q in range(2):
                            s, j = 1 - q, t2 * 2 + (first + 1 + q)
                            expo(j)
                            store(1 - s, j - 1, t2 + first // 2)
                            copy_act(s, j)
                    expo(last)
                    store(0, last - 1, last // 2)
                    copy_act(1, last)
                    store(1, last, last // 2)

                finish_tiles(0, MAIN)
                signal("slots").wait(act, "over")
                with act.If(act.value_load(over_i[0:1, OVER:OVER + 1], min_val=0, max_val=OVER) > 0):
                    finish_tiles(MAIN, OVER)
                meet(act, L)
            step = Chain(act, "act_final")
            for t in range(NT):
                if t:
                    step(last)
                last = a.activation(sq2[0:rows(t)], X[0:rows(t), t, :], ACT.Square, accum_out=ssq[0:rows(t), t:t + 1])
            signal("fin_a").mark(last, "sq")
            signal("fin_d").wait(act, "var")
            step(a.activation(nln, nvar, ACT.Ln))
            signal("fin_a").mark(a.activation(nrs, nln, ACT.Exp, scale=-0.5), "rs")

        @block.vector
        def _(dve):
            v = nc.vector
            tt, ts, stt, cp = v.tensor_tensor, v.tensor_scalar, v.scalar_tensor_tensor, v.tensor_copy
            for ap in (zero[:], dts, cum, cend):
                v.memset(ap, 0.0)
            for ap in (ssq, ssq2):
                v.memset(ap, float(D_MODEL))
            dve.wait_ge(setup_loaded, 48)
            first = Chain(dve, "dve_first")
            first(ts(neg[:, 0:P], C("upto"), 1.0, BIG, ALU.subtract, ALU.mult))
            first(ts(neg[:, P:P + NSAMP], C("upto_s"), 1.0, BIG, ALU.subtract, ALU.mult))
            first(cp(ident16[:], C("ident")))
            v.memset(sqj, 0.0).then_inc(setup_made, 1)
            dve.wait_ge(setup_made, 1)

            with dve.Fori(0, DEPTH) as L:
                step = Chain(dve, "dve_step")

                def refine(key, p, va, rs, nt, out):
                    signal("rs0").wait(dve, key)
                    step(tt(nt[0:p], va[0:p], rs[0:p], ALU.mult))
                    step(tt(nt[0:p], nt[0:p], rs[0:p], ALU.mult))
                    step(ts(nt[0:p], nt[0:p], -0.5, 1.5, ALU.mult, ALU.add))
                    step(tt(out[0:p], nt[0:p], rs[0:p], ALU.mult))

                def heads(ap, h, w):
                    return ap.rearrange("p (h w) -> p h w", h=h)

                signal("state_zero").mark(v.memset(S_ret, 0.0), "ret")
                signal("state_zero").wait(dve, "ret")
                signal("sq").wait(dve, NT - 1)
                signal("var").mark(ts(nvar, ssq, 1.0 / D_MODEL, EPS, ALU.mult, ALU.add), "n1")
                signal("var").wait(dve, "n1")
                refine("n1", P, nvar, nrs, nnt, nrms)
                signal("g1").wait(dve, "in")
                for t in range(NT + 1):
                    if t < NT:
                        n = rows(t)
                        if t >= 2:
                            banks[3].wait(dve, ("hT", t - 2, 1))
                        signal("hn").mark(ts(hn[0:n, t % 2, :], X[0:n, t, :], nrms[0:n, t:t + 1], None, ALU.mult), t)
                    if t >= 1:
                        n = rows(t - 1)
                        for h in range(2):
                            b = banks[2 + h]
                            b.wait(dve, ("hT", t - 1, h))
                            b.release(tt(hT[:, 4 * h:4 * h + 4, tok(t - 1)], heads(b.ap, 4, P)[:, :, 0:n],
                                         bc(g1[:, 4 * h:4 * h + 4], n), ALU.mult), ("hT", t - 1, h))
                signal("rope").wait(dve, "in")
                for g in range(16):
                    i, half = g // 2, g % 2
                    cols = slice(half * HALF, half * HALF + HALF)
                    b = banks[g % 2]
                    b.wait(dve, ("qk", g))
                    signal("xsw").wait(dve, g)
                    tt(rot1[:, g % 2, :], b.ap[:, 0:HALF], rope[:, 0, cols], ALU.mult)
                    b.release(tt(rot2[:, g % 2, :], xsw[:, g % 2, :], rope[:, 1, cols], ALU.mult), ("qk", g))
                    b.wait_freed(dve, ("qk", g))
                    signal("qk").mark(tt(qk[:, i, cols], rot1[:, g % 2, :], rot2[:, g % 2, :], ALU.add), g)

                signal("vectors").wait(dve, "in")

                def onT_out(t):
                    n = rows(t)
                    banks[3].wait(dve, ("onT", t))
                    banks[3].release(tt(onT[:, :, tok(t)], heads(bk[3], 4, P)[:, :, 0:n], bc(gnT, n), ALU.mult), ("onT", t))

                for t in range(NT):
                    n = rows(t)
                    sfx = "" if t < SAMPLE else "_s"
                    if t >= 2:
                        banks[7].wait(dve, ("kv", t - 2))
                    banks[2].wait(dve, ("ktok", t))
                    banks[2].release(tt(heads(ktok[0:n, t % 2, :], 4, DK), heads(bk[2][0:n, :], 4, DK), bc(C("kdec" + sfx, n), DK), ALU.mult), ("ktok", t))
                    banks[4].wait(dve, ("scores", t))
                    banks[4].release(tt(sc[0:n, t % 2, 0:4 * n], bk[4][0:n, 0:4 * n], C("decay" + sfx, n), ALU.mult), ("scores", t))
                    signal("erg").wait(dve, t)
                    e = erg[0:n, t % 2, :]
                    step(ts(e, e, 1.0, None, ALU.add))
                    step(v.reciprocal(e, e))
                    banks[1].release(tt(rgs[0:n, t % 2, :], bk[1][0:n, :], e, ALU.mult), ("rg", t))
                    o, c = ret_o[0:n], ret_c[0:n]
                    banks[6].wait(dve, ("inter", t))
                    banks[6].release(tt(heads(o, 4, DV), heads(bk[6][0:n, :], 4, DV), bc(C("qdec" + sfx, n), DV), ALU.mult), ("inter", t))
                    banks[6].wait_freed(dve, ("inter", t))
                    banks[5].wait(dve, ("intra", t))
                    banks[5].release(tt(o, o, bk[5][0:n, :], ALU.add), ("intra", t))
                    if t < SAMPLE:
                        banks[7].wait(dve, ("kv", t))
                        for h in range(H_RET):
                            hs = slice(h * DV, (h + 1) * DV)
                            last = stt(S_ret[:, hs], S_ret[:, hs], G[h] ** P, bk[7][:, hs], ALU.mult, ALU.add)
                        banks[7].release(last, ("kv", t))
                    else:
                        for h in range(H_RET):
                            for q in range(2):
                                b = banks[(7, 4)[q]]
                                b.wait(dve, ("kvs", h, q))
                                sl = natR[:, 4 * q:4 * q + 4, h, :]
                                b.release(stt(sl, sl, G[h] ** DEC_S, heads(b.ap, 4, DV), ALU.mult, ALU.add), ("kvs", h, q))
                    banks[5].wait_freed(dve, ("intra", t))
                    step(v.tensor_reduce(gsum[0:n], heads(o, 4, DV), AX.X, ALU.add))
                    step(ts(gsum[0:n], gsum[0:n], 1.0 / DV, None, ALU.mult))
                    step(tt(heads(c, 4, DV), heads(o, 4, DV), bc(gsum[0:n], DV), ALU.subtract))
                    step(tt(o, c, c, ALU.mult))
                    step(v.tensor_reduce(gvar[0:n], heads(o, 4, DV), AX.X, ALU.add))
                    signal("var").mark(ts(gvar[0:n], gvar[0:n], 1.0 / DV, EPS, ALU.mult, ALU.add), ("gn", t))
                    signal("var").wait(dve, ("gn", t))
                    refine(("gn", t), n, gvar, grs, gnt, grms)
                    step(tt(heads(c, 4, DV), heads(c, 4, DV), bc(grms[0:n], DV), ALU.mult))
                    if t >= 1:
                        onT_out(t - 1)
                    banks[1].wait_freed(dve, ("rg", t))
                    signal("gated").mark(tt(ret_q[0:n], c, rgs[0:n, t % 2, :], ALU.mult), t)
                onT_out(SAMPLE)

                step(v.memset(S_ssm, 0.0))
                for par in range(2):
                    step(v.memset(xr[:, par, 0:CONV_K - 1], 0.0))
                signal("state_zero").mark(v.memset(conv[64:128, 9, :], 0.0), "ssm")
                step(v.memset(conv[0:64, 10, :], 0.0))

                def samp(ap, w):
                    return ap.rearrange("p (b r) -> p b r", b=DEC_B, r=w)

                for g in range(NCT + 1):
                    if g < NCT:
                        for h in range(2):
                            banks[h].wait_freed(dve, ("x", g, h))
                        pr, out = xr[:, g % 2, :], cb_[:, g % 2, :]
                        sa = samp(pr[:, 3 + SEQ:], DEC_S + 3)
                        so = samp(out[:, SEQ:TOK], DEC_S)
                        if g >= 2:
                            signal("conv").wait(dve, g - 2)
                        for j in range(CONV_K):
                            w = conv_wT[:, g, j:j + 1]
                            if j == 0:
                                ts(out[:, 0:SEQ], pr[:, 0:SEQ], w, conv_bT[:, g:g + 1], ALU.mult, ALU.add)
                                last = ts(so, sa[:, :, 0:DEC_S], w, conv_bT[:, g:g + 1], ALU.mult, ALU.add)
                            else:
                                stt(out[:, 0:SEQ], pr[:, j:j + SEQ], w, out[:, 0:SEQ], ALU.mult, ALU.add)
                                last = stt(so, sa[:, :, j:j + DEC_S], w, so, ALU.mult, ALU.add)
                            if j < CONV_K - 1:
                                step(last)
                        signal("lin").mark(last, g)
                    if g >= 1:
                        k = g - 1
                        signal("ce").wait(dve, k)
                        e, c = ce[:, k % 2, :], cb_[:, k % 2, :]
                        step(ts(e, e, 1.0, None, ALU.add))
                        step(v.reciprocal(e, e))
                        if k < 9:
                            last = tt(conv[:, k, :], c, e, ALU.mult)
                        else:
                            tt(conv[0:64, 9, :], c[0:64], e[0:64], ALU.mult)
                            last = tt(conv[64:128, 10, :], c[64:128], e[64:128], ALU.mult)
                        signal("conv").mark(last, k)

                signal("head_vectors").wait(dve, "in")
                banks[3].wait(dve, ("dt",))
                dps = bk[3][:, 0:NT * H_SSD].rearrange("p (t h) -> p t h", t=NT)
                tt(dts[:, 0:SAMPLE, :], dps[:, 0:SAMPLE, :], bm(dtb, SAMPLE), ALU.add)
                banks[3].release(tt(dts[0:NSAMP, SAMPLE, :], dps[0:NSAMP, SAMPLE, :], dtb[0:NSAMP], ALU.add), ("dt",))
                banks[3].wait_freed(dve, ("dt",))
                step(ts(dt1, dts, -1.0, None, ALU.mult))
                signal("sp").mark(tt(dt1, dt1, dts, ALU.min), "arg")
                signal("spa").wait(dve, "e")
                signal("sp").mark(ts(dt1, dt2, 1.0, None, ALU.add), "u")
                signal("sp").wait(dve, "u")
                step(ts(cum, dt1, -1.0, 1e-30, ALU.add, ALU.max))
                step(v.reciprocal(cum, cum))
                step(tt(cum, cum, dt2, ALU.mult))
                signal("spa").wait(dve, "ln")
                step(tt(cum, cum, dt3, ALU.mult))
                step(stt(dt3, dt1, 1.0, dt2, ALU.is_equal, ALU.mult))
                step(tt(cum, cum, dt3, ALU.add))
                step(stt(dts, dts, 0.0, cum, ALU.max, ALU.add))
                signal("acoef").wait(dve, 0)
                step(ts(acoef, acoef, -1.0, None, ALU.mult))
                step(tt(dta, dts, bm(acoef, NT), ALU.mult))
                step(v.memset(cum, 0.0))
                signal("dta").mark(v.memset(cend, 0.0), 0)
                banks[3].wait(dve, ("cum",))
                signal("dta").wait(dve, 0)
                cps = bk[3][:, 0:NT * 32].rearrange("p (t h) -> p t h", t=NT)
                for dst, off in ((cum, 0), (cend, 16)):
                    cp(dst[:, 0:SAMPLE, :], cps[:, 0:SAMPLE, off:off + 16])
                    last = cp(dst[0:NSAMP, SAMPLE, :], cps[0:NSAMP, SAMPLE, off:off + 16])
                banks[3].release(last, ("cum",))
                banks[3].wait_freed(dve, ("cum",))
                ts(ncum, cum, -1.0, None, ALU.mult)
                signal("decays").mark(tt(wend, cend, cum, ALU.subtract), "args")
                signal("decayed").wait(dve, 0)

                def yT_out(t):
                    n = rows(t)
                    if t == 0:
                        for key in ("retp", "convp", "convs"):
                            signal("out_" + key).wait(dve, "out")
                    for h in range(2):
                        b = banks[h]
                        b.wait(dve, ("yT", t, h))
                        b.release(tt(yT[:, 4 * h:4 * h + 4, tok(t)], heads(b.ap, 4, P)[:, :, 0:n], bc(sngT[:, 4 * h:4 * h + 4], n), ALU.mult), ("yT", t, h))

                signal("out_retp").wait(dve, "out")
                signal("head_vectors").wait(dve, "in")
                step(v.memset(btz, 0.0))
                for t in range(NT):
                    n = rows(t)
                    if t:
                        banks[3].wait(dve, ("yin", t - 1, 1))
                        signal("wx").wait(dve, t - 1)
                    for h in range(2):
                        b = banks[2 + h]
                        b.wait(dve, ("xsT", t, h))
                        signal("xs").wait(dve, (t, h))
                        b.release(tt(heads(xdt[0:n, 512 * h:512 * h + 512], 8, 64), heads(b.ap[0:n, :], 8, 64), bc(dts[0:n, t, 8 * h:8 * h + 8], 64), ALU.mult), ("xsT", t, h))
                    banks[4].wait(dve, ("cb", t))
                    if t:
                        banks[7].wait(dve, ("bx", t - 1))
                    for g in range(2):
                        last = cp(btz[0:n, g, 64 * g:64 * g + 64], bk[4][0:n, 256 + 64 * g:320 + 64 * g])
                    signal("btz").mark(last, t)
                    if t == SAMPLE:
                        signal("out_ssmp").wait(dve, "out")
                    for h in range(2):
                        hs = slice(512 * h, 512 * h + 512)
                        signal("ez").wait(dve, (t, h))
                        step(ts(ez[0:n, hs], ez[0:n, hs], 1.0, None, ALU.add))
                        step(v.reciprocal(ez[0:n, hs], ez[0:n, hs]))
                        banks[h].release(tt(zs[0:n, hs], bk[h][0:n, :], ez[0:n, hs], ALU.mult), ("z", t, h))
                    for r in range(4):
                        b = banks[5 + r % 2]
                        b.wait_freed(dve, ("seg", t, r))
                        w = wl[0:n, 4 * r * n:4 * (r + 1) * n].rearrange("p (h m) -> p h m", h=4)
                        last = tt(w, w, bm(bk[4][0:n, (r // 2) * n:(r // 2 + 1) * n], 4), ALU.mult)
                    banks[4].release(last, ("cb", t))
                    if t == SAMPLE:
                        for g in range(2):
                            if g:
                                banks[4].wait(dve, ("bxs", 3))
                            else:
                                signal("btz").wait(dve, t)
                                banks[1].wait_freed(dve, ("z", t, 1))
                            signal("bexp").mark(tt(heads(bexp[0:n], 8, 64), bm(btz[0:n, g, 64 * g:64 * g + 64], 8), bc(C("seqcol", n), 64), ALU.mult), g)
                            for c in range(4 * g, 4 * g + 4):
                                b = banks[(7, 4)[c % 2]]
                                if c == 0:
                                    banks[7].wait_freed(dve, ("e8",))
                                old = natS[:, :, c % 4, c // 4, :]
                                step(tt(old, old, bc(E8[:, c, :], 64), ALU.mult))
                                b.wait(dve, ("bxs", c))
                                b.release(tt(old, old, heads(b.ap, 8, 64), ALU.add), ("bxs", c))
                    if t:
                        banks[1].wait(dve, ("yT", t - 1, 1))
                    for g in range(2):
                        gs = slice(512 * g, 512 * g + 512)
                        banks[5 + g].wait(dve, ("yst", t, g))
                        banks[5 + g].release(tt(heads(yb[0:n, gs], 8, 64), heads(bk[5 + g][0:n, :], 8, 64), bc(ecum[0:n, t, 8 * g:8 * g + 8], 64), ALU.mult), ("yst", t, g))
                    if t < SAMPLE:
                        banks[7].wait(dve, ("bx", t))
                        for g in range(2):
                            gp = slice(64 * g, 64 * g + 64)
                            last = tt(heads(S_ssm[gp], 8, 64), heads(S_ssm[gp], 8, 64), bc(dec[gp, t, 8 * g:8 * g + 8], 64), ALU.mult)
                        step(last)
                        banks[7].release(tt(S_ssm, S_ssm, bk[7], ALU.add), ("bx", t))
                    for g in range(2):
                        gs = slice(512 * g, 512 * g + 512)
                        banks[5 + g].wait_freed(dve, ("yst", t, g))
                        banks[2 + g].wait(dve, ("yin", t, g))
                        banks[2 + g].release(tt(yb[0:n, gs], yb[0:n, gs], bk[2 + g][0:n, :], ALU.add), ("yin", t, g))
                    signal("xsd").wait(dve, t)
                    banks[3].wait_freed(dve, ("yin", t, 1))
                    signal("ylin").mark(tt(yb[0:n], yb[0:n], xs[0:n], ALU.add), t)
                    signal("ylin").wait(dve, t)
                    banks[1].wait_freed(dve, ("z", t, 1))
                    signal("yz").mark(tt(yb[0:n], yb[0:n], zs[0:n], ALU.mult), t)
                    if t:
                        yT_out(t - 1)
                    signal("ysq").wait(dve, t)
                    signal("var").mark(ts(yvar[0:n], ysum[0:n], 1.0 / 512, EPS, ALU.mult, ALU.add), ("y", t))
                    signal("var").wait(dve, ("y", t))
                    refine(("y", t), n, yvar, yrs, ynt, yrms)
                    signal("y").mark(tt(heads(yb[0:n], 2, 512), heads(yb[0:n], 2, 512), bc(yrms[0:n], 512), ALU.mult), t)
                yT_out(SAMPLE)

                for g in range(32):
                    c, half = (g // 2) % 8, g % 2
                    cols = slice(half * HALF, half * HALF + HALF)
                    banks[g % 2].wait_freed(dve, ("gate", g))
                    e = ge[:, g % 2, :]
                    step(ts(e, e, 1.0, None, ALU.add))
                    step(v.reciprocal(e, e))
                    b = banks[2 + g % 2]
                    b.wait(dve, ("branch", g))
                    if g < 16:
                        b.release(tt(mT[:, c, cols], e, b.ap[:, 0:HALF], ALU.mult), ("branch", g))
                    else:
                        b.release(tt(mix2, e, b.ap[:, 0:HALF], ALU.mult), ("branch", g))
                        b.wait_freed(dve, ("branch", g))
                        signal("mix").mark(tt(mT[:, c, cols], mT[:, c, cols], mix2, ALU.add), g)

                signal("x_spilled").wait(dve, "in")
                for t in range(NT):
                    n = rows(t)
                    for h in range(2):
                        b = banks[4 + (2 * t + h) % 4]
                        b.wait(dve, ("wo", t, h))
                        xx = X[0:n, t, 512 * h:512 * h + 512]
                        b.release(tt(xx, xx, b.ap[0:n, :], ALU.add), ("wo", t, h))
                signal("sq2").wait(dve, NT - 1)
                signal("var").mark(ts(nvar2, ssq2, 1.0 / D_MODEL, EPS, ALU.mult, ALU.add), "n2")
                signal("var").wait(dve, "n2")
                refine("n2", P, nvar2, nrs2, nnt2, nrms2)
                for key in ("ssmp", "ssms"):
                    signal("out_" + key).wait(dve, "out")
                for t in range(NT):
                    n = rows(t)
                    signal("xn").mark(ts(xn[0:n, t, :], X[0:n, t, :], nrms2[0:n, t:t + 1], None, ALU.mult), t)
                for t in range(NT):
                    n = rows(t)
                    if t >= 2:
                        signal("routed").wait(dve, t - 2)
                    for h in range(2):
                        b = banks[2 + h]
                        b.wait(dve, ("tT", t, h))
                        b.release(tt(tT[:, t % 2, 4 * h:4 * h + 4, 0:n], heads(b.ap, 4, P)[:, :, 0:n], bc(g2[:, 4 * h:4 * h + 4], n), ALU.mult), ("tT", t, h))

                for ap in (glog, elog, rank):
                    step(v.memset(ap, 0.0))
                banks[0].wait(dve, ("router",))
                rps = bk[0][:, 0:NT * 20].rearrange("p (t e) -> p t e", t=NT)
                for dst, a, z in ((glog, 0, 4), (elog, 4, 20)):
                    cp(dst[:, 0:SAMPLE, :], rps[:, 0:SAMPLE, a:z])
                    last = cp(dst[0:NSAMP, SAMPLE, :], rps[0:NSAMP, SAMPLE, a:z])
                banks[0].release(last, ("router",))
                banks[0].wait_freed(dve, ("router",))

                def top(val, best, back, scratch, idx, hot):
                    n = val.shape[2]
                    step(v.tensor_reduce(best, val, AX.X, ALU.max))
                    step(tt(scratch, val, bc(best, n), ALU.is_equal))
                    step(tt(scratch, scratch, bm(C(back), NT), ALU.mult))
                    step(v.tensor_reduce(idx, scratch, AX.X, ALU.min))
                    step(tt(hot, bm(C(back), NT), bc(idx, n), ALU.is_equal))

                step(v.tensor_reduce(gmax, glog, AX.X, ALU.max))
                signal("route").mark(tt(r4a, glog, bc(gmax, N_GRP), ALU.subtract), "gd")
                signal("routea").wait(dve, "g")
                step(v.tensor_reduce(gden, r4b, AX.X, ALU.add))
                step(v.reciprocal(gden, gden))
                top(glog, gmax, "back4", r4b, gidx, r4a)
                step(ts(r4b, r4a, 1.0, BIG, ALU.subtract, ALU.mult))
                step(tt(ra.rearrange("p t (g e) -> p (t g) e", g=N_GRP), elog.rearrange("p t (g e) -> p (t g) e", g=N_GRP),
                        bc(r4b.rearrange("p t g -> p (t g)"), EXP_PG), ALU.add))
                top(ra, m1, "back16", rb, i1, oh1)
                step(stt(ra, oh1, -BIG, ra, ALU.mult, ALU.add))
                top(ra, m2, "back16", rb, i2, oh2)
                signal("route").mark(tt(rt1, m2, m1, ALU.subtract), "ed")
                step(tt(hit, oh1, oh2, ALU.add))
                signal("hit").mark(tt(hit, hit, bc(C("valid"), N_EXP), ALU.mult), 0)
                signal("routea").wait(dve, "e")
                step(ts(rt3, rt2, 1.0, None, ALU.add))
                step(v.reciprocal(rt3, rt3))
                step(tt(w1, rt3, gden, ALU.mult))
                step(tt(w2, w1, rt2, ALU.mult))
                banks[1].wait(dve, ("rank",))
                kps = bk[1][:, 0:80].rearrange("p (t e) -> p t e", t=NT)
                cp(rank[:, 0:SAMPLE, :], kps[:, 0:SAMPLE, :])
                cp(rank[0:NSAMP, SAMPLE, :], kps[0:NSAMP, SAMPLE, :])
                banks[1].release(cp(tot, bk[1][:, 80:96]), ("rank",))
                banks[1].wait_freed(dve, ("rank",))
                step(ts(otile, tot, float(MAIN_CAP), None, ALU.is_gt))
                for k in range(1, (TOK - MAIN_CAP - 1) // CAP + 1):
                    step(stt(otile, tot, float(MAIN_CAP + CAP * k), otile, ALU.is_gt, ALU.add))
                step(cp(oscan, otile))
                for k in (1, 2, 4, 8):
                    step(cp(oend, oscan))
                    step(tt(oscan[:, k:], oend[:, k:], oend[:, 0:N_EXP - k], ALU.add))
                step(tt(obase, oscan, otile, ALU.subtract))
                step(ts(oend, obase, float(CAP), float(MAIN * CAP - MAIN_CAP), ALU.mult, ALU.add))
                step(tt(ra, rank, bm(C("slot0"), NT), ALU.add))
                step(tt(rb, rank, bm(oend, NT), ALU.add))
                step(tt(ra, ra, rb, ALU.subtract))
                step(stt(ra, rank, float(MAIN_CAP), ra, ALU.is_lt, ALU.mult))
                step(tt(slot_e, ra, rb, ALU.add))
                for c, oh in enumerate((oh1, oh2)):
                    step(tt(ra, oh, slot_e, ALU.mult))
                    step(v.tensor_reduce(slots_f[:, c, :], ra, AX.X, ALU.add))
                signal("slots").mark(cp(slot_i[:], slots_f.rearrange("p c t -> p (c t)")), 0)
                step(tt(ov_a, bc(C("overno"), N_EXP), bm(obase, OVER), ALU.is_ge))
                step(tt(ov_b, bc(C("overno"), N_EXP), bm(oscan, OVER), ALU.is_lt))
                step(tt(ov_a, ov_a, ov_b, ALU.mult))
                step(tt(ov_a, ov_a, bm(C("expno"), OVER), ALU.mult))
                step(v.tensor_reduce(ov_c, ov_a, AX.X, ALU.add))
                cp(over_i[:, OVER:OVER + 1], oscan[:, N_EXP - 1:N_EXP])
                signal("slots").mark(cp(over_i[:, 0:OVER], ov_c), "over")

                def act_tile(s, j):
                    dve.sem_clear(moe_chain)
                    dve.wait_ge(sig_e, j + 1)
                    ts(fe, fe, 1.0, None, ALU.add).then_inc(moe_chain, 1)
                    dve.wait_ge(moe_chain, 1)
                    v.reciprocal(fe, fe).then_inc(moe_chain, 1)
                    dve.wait_ge(moe_chain, 2)
                    if not isinstance(j, int) or j > 1:
                        dve.wait_ge(act_T, j - 1)
                    tt(fa[:, s, :], bk[0], fe, ALU.mult).then_inc(moe_chain, 1)
                    dve.wait_ge(moe_chain, 3)
                    tt(fa[:, s, :], fa[:, s, :], bk[1], ALU.mult).then_inc(acted, 1)

                def copy_rows(s, j):
                    dve.wait_ge(x_T, j + 1)
                    if not isinstance(j, int) or j > 1:
                        dve.wait_ge(gate_up, j - 1)
                    for h in range(2):
                        last = tt(xsT[:, s, 4 * h:4 * h + 4, :], heads(bk[2 + h], 4, P), bc(g2[:, 4 * h:4 * h + 4], P), ALU.mult)
                    last.then_inc(x_Tc, 1)

                def activate_tiles(first, count):
                    copy_rows(0, first)
                    copy_rows(1, first + 1)
                    act_tile(0, first)
                    with dve.Fori(0, (count - 2) // 2) as t2:
                        for q in range(2):
                            s = 1 - q
                            act_tile(s, t2 * 2 + (first + 1 + q))
                            copy_rows(1 - s, t2 * 2 + (first + 2 + q))
                    act_tile(1, first + count - 1)

                activate_tiles(0, MAIN)
                signal("slots").wait(dve, "over")
                with dve.If(dve.value_load(over_i[0:1, OVER:OVER + 1], min_val=0, max_val=OVER) > 0):
                    activate_tiles(MAIN, OVER)

                for c, w in enumerate((w1, w2)):
                    for t in range(NT):
                        n = rows(t)
                        dve.wait_ge(gathered[c * NT + t], L * 16 + 16)
                        step(stt(X[0:n, t, :], got[0:n, c * NT + t, :], w[0:n, t:t + 1], X[0:n, t, :], ALU.mult, ALU.add))
                meet(dve, L)

            step = Chain(dve, "dve_final")
            signal("fin_a").wait(dve, "sq")
            signal("fin_d").mark(ts(nvar, ssq, 1.0 / D_MODEL, EPS, ALU.mult, ALU.add), "var")
            signal("fin_d").wait(dve, "var")
            signal("fin_a").wait(dve, "rs")
            step(tt(nnt, nvar, nrs, ALU.mult))
            step(tt(nnt, nnt, nrs, ALU.mult))
            step(ts(nnt, nnt, -0.5, 1.5, ALU.mult, ALU.add))
            step(tt(nrms, nnt, nrs, ALU.mult))
            dve.wait_ge(final_loaded, 16)
            for t in range(NT):
                n = rows(t)
                last = stt(xn[0:n, t, :], X[0:n, t, :], nrms[0:n, t:t + 1], gf[0:n], ALU.mult, ALU.mult)
            last.then_inc(final_made, 1)

        @block.gpsimd
        def _(pool):
            g_ = nc.gpsimd
            pool.wait_ge(setup_made, 1)
            pool.wait_ge(slot_loaded[1], 16)
            for i in range(TILES):
                pool.dma_start(slot_in[i * P:(i + 1) * P, :].rearrange("p (c x) -> p c x", c=4), bm(zero[:], 4)).then_inc(zeroed, 16)
            for i in range(MAIN, TILES):
                pool.dma_start(slot_out[i * P:(i + 1) * P, :].rearrange("p (c x) -> p c x", c=4), bm(zero[:], 4)).then_inc(zeroed, 16)
            pool.wait_ge(zeroed, 16 * (TILES + OVER))
            with pool.Fori(0, DEPTH) as L:
                signal("qk").wait(pool, 15)
                seqrow = C("seqrow").rearrange("p (b m) -> p b m", b=DEC_B)
                for h in range(H_RET):
                    signal("qexp").mark(g_.tensor_tensor(qexp[:, h, :].rearrange("p (b m) -> p b m", b=DEC_B), bm(qk[:, h, tok(SAMPLE)], DEC_B), seqrow, ALU.mult), h)
                banks[0].wait_freed(pool, ("v", SAMPLE))
                for h in range(H_RET):
                    if h:
                        banks[4].wait(pool, ("kvs", h - 1, 1))
                    signal("vexp").mark(g_.tensor_tensor(vexp[0:NSAMP], bm(vt[0:NSAMP, SAMPLE % 2, h * DV:(h + 1) * DV], DEC_B),
                                                         bc(C("seqcol", NSAMP), DV), ALU.mult), h)
                signal("gated").wait(pool, SAMPLE)
                for g in range(NCT):
                    for h in range(2):
                        banks[h].wait_freed(pool, ("x", g, h))
                    g_.tensor_copy(cvo[:, g, 0:3], xr[:, g % 2, SEQ:SEQ + 3])
                    signal("cvo").mark(g_.tensor_copy(cvo[:, g, 3:27].rearrange("p (b r) -> p b r", b=DEC_B),
                                                      xr[:, g % 2, 3 + SEQ:].rearrange("p (b r) -> p b r", b=DEC_B)[:, :, DEC_S:]), g)
                signal("head_vectors").wait(pool, "in")
                signal("dta").wait(pool, 0)
                signal("decayed").wait(pool, 0)
                signal("conv").wait(pool, NCT - 1)
                for q in range(3):
                    banks[4 + q].wait(pool, ("cvo", q))
                for t in range(NT):
                    n = rows(t)

                    def udo(r):
                        if r >= 2 or t:
                            banks[5 + r % 2].wait(pool, ("seg", t, r - 2) if r >= 2 else ("seg", t - 1, r + 2))
                        m = C("upto" if t < SAMPLE else "upto_s", n)
                        signal("ud").mark(g_.tensor_tensor(ud[0:n, r % 2, 0:4 * n].rearrange("p (h m) -> p h m", h=4), bm(m, 4),
                                                           bc(dta[0:n, t, 4 * r:4 * r + 4], n), ALU.mult), (t, r))
                    udo(0)
                    udo(1)
                    for h in range(2):
                        banks[2 + h].wait_freed(pool, ("xsT", t, h))
                    if t:
                        banks[7].wait(pool, ("bx", t - 1))
                    signal("wx").mark(g_.tensor_tensor(wx[0:n].rearrange("p (h w) -> p h w", h=H_SSD), xdt[0:n].rearrange("p (h w) -> p h w", h=H_SSD),
                                                       bc(wend[0:n, t, :], 64), ALU.mult), t)
                    signal("xsd").mark(g_.tensor_tensor(xs[0:n].rearrange("p (h w) -> p h w", h=H_SSD), xs[0:n].rearrange("p (h w) -> p h w", h=H_SSD),
                                                        bc(dskip[0:n], 64), ALU.mult), t)
                    udo(2)
                    udo(3)
                    if t == SAMPLE:
                        banks[3].wait(pool, ("yin", t - 1, 1))
                        for g in range(2):
                            signal("czexp").mark(g_.tensor_tensor(czexp[:, 512 * g:512 * g + 512].rearrange("p (b m) -> p b m", b=DEC_B),
                                                                  bm(conv[:, 9 + g, tok(t)], DEC_B), seqrow, ALU.mult), g)
                        banks[6].wait(pool, ("seg", t, 3))
                        signal("dtx").mark(g_.tensor_copy(dtx[0:n].rearrange("p (h w) -> p h w", h=H_SSD), bc(dta[0:n, t, :], 64)), 0)
                signal("slots").wait(pool, 0)
                signal("xn").wait(pool, NT - 1)
                for c in range(2):
                    for t in range(NT):
                        n = rows(t)
                        g_.indirect_dma_start(slot_in, bass.IndirectOffsetOnAxis(ap=slot_i[0:n, c * NT + t:c * NT + t + 1], axis=0),
                                              xn[0:n, t, :], None).then_inc(scattered, 16)
                pool.wait_ge(scattered, L * (32 * NT) + 32 * NT)
                pool.sem_inc(aside, 1)
                signal("slots").wait(pool, "over")
                signal("rows_ready").mark(g_.memset(mark_row, 0.0), "all")
                for s in range(2):
                    pool.wait_ge(out_stored[s], 16 + 16 * (MAIN // 2))
                with pool.If(pool.value_load(over_i[0:1, OVER:OVER + 1], min_val=0, max_val=OVER) > 0):
                    for s in range(2):
                        pool.wait_ge(out_stored[s], 16 + 16 * (TILES // 2))
                for c in range(2):
                    for t in range(NT):
                        n = rows(t)
                        g_.indirect_dma_start(got[0:n, c * NT + t, :], None, slot_out,
                                              bass.IndirectOffsetOnAxis(ap=slot_i[0:n, c * NT + t:c * NT + t + 1], axis=0)).then_inc(gathered[c * NT + t], 16)
                meet(pool, L)

    plan["names"] = list(signals)


_INS = ["x_prompt", "x_sample", "state_ret", "state_ssm", "state_conv", "ln1_g", "w_in", "ret_gn_g", "w_ret_out",
        "conv_w", "conv_b", "dt_bias", "a_log", "d_skip", "ssd_norm_g", "w_ssd_out", "w_o", "ln2_g",
        "w_router_group", "w_router_expert", "w_e_gate", "w_e_up", "w_e_down", "lnf_g"]
_OUTS = [(1, SEQ, D_MODEL), (DEC_B, DEC_S, D_MODEL), (DEPTH, 1, H_RET, DK, DV), (DEPTH, 1, H_SSD, P_SSD, N_SSD),
         (DEPTH, 1, CONV_K - 1, CONV_DIM), (DEPTH, DEC_B, H_RET, DK, DV), (DEPTH, DEC_B, H_SSD, P_SSD, N_SSD),
         (DEPTH, DEC_B, CONV_K - 1, CONV_DIM)]


def kernel(**inputs):
    import numpy as _np
    import concourse.bacc as _bacc
    from concourse import mybir as _mybir
    from concourse.bass_utils import run_bass_kernel_spmd as _run

    arrays = {f"in_{name}": _np.ascontiguousarray(inputs[name]) for name in _INS}
    arrays["in_table"] = _np.concatenate(list(constants().values()), 1)
    plan = {}
    for _ in range(2):
        nc = _bacc.Bacc("TRN2", target_bir_lowering=False, num_devices=1)
        args = [nc.dram_tensor(n, a.shape, _mybir.dt.from_np(a.dtype), kind="ExternalInput").ap() for n, a in arrays.items()]
        args += [nc.dram_tensor(f"out_{i}", shape, _mybir.dt.float32, kind="ExternalOutput").ap() for i, shape in enumerate(_OUTS)]
        build(nc, plan, *args)
    r = _run(nc, [arrays], core_ids=[0])
    return tuple(r.results[0][f"out_{i}"] for i in range(len(_OUTS)))
```

```python
from contextlib import ExitStack

import numpy as np

import concourse.bass as bass
from concourse import mybir

F32 = mybir.dt.float32
BF16 = mybir.dt.bfloat16
I32 = mybir.dt.int32
ALU = mybir.AluOpType
ACT = mybir.ActivationFunctionType
AX = mybir.AxisListType

P = 128
DEPTH, D_MODEL = 2, 1024
SEQ, DEC_B, DEC_S, PAST = 512, 8, 8, 4096
NSAMP = DEC_B * DEC_S
TOK = SEQ + NSAMP
NT = SEQ // P + 1
SAMPLE = NT - 1
KD = D_MODEL // P
H_RET, DK, DV = 4, 128, 128
RET_W = H_RET * DV
H_SSD, P_SSD, G_SSD, N_SSD = 16, 64, 2, 64
SSD_W = H_SSD * P_SSD
CONV_K = 4
CONV_DIM = SSD_W + 2 * G_SSD * N_SSD
NCT = CONV_DIM // P
N_GRP, EXP_PG, N_EXP, D_FF = 4, 4, 16, 512
EPS = 1e-6
UNIT = 512
HALF = TOK // 2
HPRE = SEQ - HALF

COL_Q, COL_K, COL_V, COL_RG = 0, 512, 1024, 1536
COL_Z = 4 * RET_W
COL_X = COL_Z + SSD_W
COL_DT = COL_X + CONV_DIM
COL_GR = COL_DT + H_SSD
COL_GS = COL_GR + D_MODEL

CAP = P
MAIN = N_EXP
MAIN_CAP = CAP
OVER = TOK * 2 // (MAIN_CAP + 1)
TILES = MAIN + OVER
SLOTS = TILES * CAP
RING = 3
BIG = 1e30

UNITS = [("q", COL_Q, 512), ("k", COL_K, 512), ("v", COL_V, 512), ("rg", COL_RG, 512),
         ("x0", COL_X, 512), ("x1", COL_X + 512, 512), ("x2", COL_X + 1024, 256),
         ("z0", COL_Z, 512), ("z1", COL_Z + 512, 512),
         ("gr0", COL_GR, 512), ("ro0", 0, 512), ("gr1", COL_GR + 512, 512), ("ro1", 512, 512),
         ("gs0", COL_GS, 512), ("so0", 0, 512), ("gs1", COL_GS + 512, 512), ("so1", 512, 512),
         ("wo0", 0, 512), ("wo1", 512, 512)]
UNIT_NO = {u[0]: i for i, u in enumerate(UNITS)}
MOE_SLOT = [(len(UNITS) + i) % RING for i in range(RING)]
PHASE_USES = [len(range(s, len(UNITS), RING)) for s in MOE_SLOT]


def rows(t):
    return P if t < SAMPLE else NSAMP


def tok(t):
    return slice(P * t, P * t + rows(t))


def gammas():
    return 1.0 - 2.0 ** (-5.0 - np.arange(H_RET))


def constants():
    i = np.arange(P)
    g = gammas()
    scale = DK ** -0.5
    c = {"ident": np.eye(P), "upto": (i[:, None] <= i[None, :]), "before": (i[:, None] < i[None, :]), "ones": np.ones((P, P))}
    same = (i[:, None] // DEC_S == i[None, :] // DEC_S)
    up_s = (same & (i[:, None] <= i[None, :]))[:, :NSAMP]
    c["upto_s"] = up_s
    c["ones_s"] = same[:, :NSAMP]
    rel = (i[None, :] - i[:, None])
    c["decay"] = np.concatenate([np.where(rel >= 0, x ** np.maximum(rel, 0), 0) * scale for x in g], 1)
    c["decay_s"] = np.concatenate([np.where(up_s, x ** np.maximum(rel[:, :NSAMP], 0), 0) * scale for x in g], 1)
    c["kdec"] = scale * g[None, :] ** (P - 1 - i[:, None])
    c["kdec_s"] = scale * g[None, :] ** (DEC_S - 1 - i[:, None] % DEC_S)
    c["qdec"] = g[None, :] ** (i[:, None] + 1)
    c["qdec_s"] = g[None, :] ** (i[:, None] % DEC_S + 1)
    seq_of = np.arange(NSAMP) // DEC_S
    c["seqrow"] = np.tile((np.arange(DEC_B)[:, None] == seq_of[None, :]).reshape(1, -1), (P, 1))
    c["seqcol"] = (i[:, None] // DEC_S == np.arange(DEC_B)[None, :])
    half = DK // 2
    pos = np.concatenate([np.arange(SEQ), PAST + np.tile(np.arange(DEC_S), DEC_B)]).astype(np.float32)
    inv = np.power(np.float32(10000.0), -np.arange(half, dtype=np.float32) / np.float32(half))
    ang = (pos[None, :] * inv[:, None]).astype(np.float64)
    c["slot0"] = np.tile(CAP * np.arange(N_EXP)[None, :], (P, 1))
    c["back16"] = np.tile(np.arange(N_EXP)[None, :] - N_EXP, (P, 1))
    c["back4"] = np.tile(np.arange(N_GRP)[None, :] - N_GRP, (P, 1))
    c["expno"] = np.tile(np.arange(N_EXP)[None, :], (P, 1))
    c["overno"] = np.tile(np.arange(OVER)[None, :], (P, 1))
    c["valid"] = (i[:, None] + P * np.arange(NT)[None, :] < TOK)
    c["cos"] = np.concatenate([np.cos(ang), np.cos(ang)], 0)
    c["sin"] = np.concatenate([-np.sin(ang), np.sin(ang)], 0)
    return {k: np.asarray(v, np.float32) for k, v in c.items()}


CONST_AT = {}
_n = 0
for _k, _v in constants().items():
    CONST_AT[_k] = (_n, _v.shape[1])
    _n += _v.shape[1]
CONST_COLS = CONST_AT["cos"][0]


class Signal:

    def __init__(self, sem, name, plan):
        self.sem, self.name, self.plan, self.total, self.seen = sem, name, plan, 0, {}
        self.last = plan.get((name, "total"), 0)

    def mark(self, ins, key, n=1):
        self.total += n
        ins.then_inc(self.sem, n)
        self.plan[self.name, key] = self.total
        self.plan[self.name, "total"] = self.total

    def wait(self, eng, key, layer=None):
        value = self.plan.get((self.name, key), 1)
        if layer is not None:
            eng.wait_ge(self.sem, layer * self.last + value)
        elif self.seen.get(id(eng), 0) < value:
            self.seen[id(eng)] = value
            eng.wait_ge(self.sem, value)


class Bank:

    def __init__(self, ap, full, free, plan, no):
        self.ap, self.full, self.free, self.plan, self.no, self.order = ap, full, free, plan, no, []
        self.given, self.seen = {}, {}

    def acquire(self, pe, key):
        need = sum(self.plan.get(("released", self.no, k), 1) for k in self.order)
        if need:
            pe.wait_ge(self.free, need)
        self.order.append(key)
        self.plan["fill", self.no, key] = len(self.order)
        self.plan["all", self.no] = [k for k in self.order]

    def filled(self, ins):
        ins.then_inc(self.full, 1)

    def wait(self, eng, key):
        eng.wait_ge(self.full, self.plan.get(("fill", self.no, key), 1))

    def release(self, ins, key):
        self.given[key] = self.given.get(key, 0) + 1
        self.plan["released", self.no, key] = self.given[key]
        ins.then_inc(self.free, 1)

    def wait_freed(self, eng, key):
        order = self.plan.get(("all", self.no), [])
        upto = order[:order.index(key) + 1] if key in order else []
        need = sum(self.plan.get(("released", self.no, k), 1) for k in upto) or 1
        if self.seen.get(id(eng), 0) < need:
            self.seen[id(eng)] = need
            eng.wait_ge(self.free, need)

    def releases(self):
        return sum(self.plan.get(("released", self.no, k), 1) for k in self.plan.get(("all", self.no), []))


def build(nc, plan, x_p, x_s, state_ret, state_ssm, state_conv, ln1_g, w_in, ret_gn_g, w_ret_out, conv_w, conv_b,
          dt_bias, a_log, d_skip, ssd_norm_g, w_ssd_out, w_o, ln2_g, w_rg, w_re, w_gate, w_up, w_down, lnf_g,
          table, y_p, y_s, ret_p, ssm_p, conv_p, ret_s, ssm_s, conv_s):
    x_spill = nc.dram_tensor("x_spill", (NT * P, D_MODEL), F32, kind="Internal").ap()
    slot_in = nc.dram_tensor("slot_in", (SLOTS, D_MODEL), F32, kind="Internal").ap()
    slot_out = nc.dram_tensor("slot_out", (SLOTS, D_MODEL), F32, kind="Internal").ap()

    with ExitStack() as ctx:
        def sb(name, *free, dt=F32):
            return ctx.enter_context(nc.sbuf_tensor(name, [P, *free], dt))

        def sem(name):
            return ctx.enter_context(nc.semaphore(name))

        signals = {}

        def signal(name):
            if name not in signals:
                signals[name] = Signal(sem(name), name, plan)
            return signals[name]

        const = sb("const", CONST_COLS)
        ring = sb("ring", RING, 8 * UNIT)
        X = sb("X", NT, D_MODEL)
        ARENA = 31936
        arena = sb("arena", ARENA)
        small = sb("small", 1350)
        zero = sb("zero", 128)
        w_dt = sb("w_dt", KD, H_SSD)
        neg = sb("neg", P + NSAMP, dt=BF16)
        ident16 = sb("ident16", P, dt=BF16)
        slot_i = sb("slot_i", 2 * NT, dt=I32)
        over_i = sb("over_i", OVER + 1, dt=I32)

        def C(name, p=P):
            a, n = CONST_AT[name]
            return const[0:p, a:a + n]

        class Carve:
            def __init__(self, tensor, at, end):
                self.t, self.at, self.end = tensor, at, end

            def __call__(self, *free):
                n = int(np.prod(free))
                a = self.t[:, self.at:self.at + n]
                self.at += n
                assert self.at <= self.end, (self.at, self.end)
                if len(free) == 1:
                    return a
                names = " ".join("abcd"[:len(free)])
                return a.rearrange(f"p ({names}) -> p {names}", **{"abcd"[i]: free[i] for i in range(len(free))})

        S = Carve(small, 0, 1350)
        A = Carve(arena, 0, ARENA)
        hT = A(KD, TOK)
        qk = A(KD + 3, TOK)
        onT = A(RET_W // P, TOK)
        yT = A(KD, TOK)
        nat = A(DEC_B * 8, 64)
        tmp0 = A.at
        conv = qk
        mT = qk[:, 0:KD, :]
        yflat = yT.rearrange("p k n -> p (k n)")
        cvn_in, cvo_n, S_ret = yflat[:, 0:1280], yflat[:, 1280:2560], yflat[:, 2560:3072]
        vexp = yflat[:, 3072:4096].rearrange("p (b v) -> p b v", b=DEC_B)
        natS = nat.rearrange("p (b h g) k -> p b h g k", b=DEC_B, g=G_SSD)
        natR = nat.rearrange("p (b h x) k -> p b h (x k)", b=DEC_B, h=H_RET)
        ssmT = X[:, 0:4, :].rearrange("p a b -> p (a b)").rearrange("p (b c) -> p b c", b=DEC_B)

        g1, g2, conv_wT, conv_bT = S(KD), S(KD), S(NCT, CONV_K), S(NCT)
        gnT, sngT = S(RET_W // P), S(KD)
        dskip, alog, dtb, acoef = S(H_SSD), S(H_SSD), S(H_SSD), S(H_SSD)
        w_router = S(KD, N_GRP + N_EXP)
        ssq, nvar, nln, nrs, nnt, nrms = (S(NT) for _ in range(6))
        ssq2, nvar2, nln2, nrs2, nnt2, nrms2 = (S(NT) for _ in range(6))
        dts, dt1, dt2, dt3, dta = (S(NT, H_SSD) for _ in range(5))
        cum, cend, ncum, ecum, wend, dec = (S(NT, H_SSD) for _ in range(6))
        gsum, gvar, gln, grs, gnt, grms = (S(4) for _ in range(6))
        ysum, yvar, yln, yrs, ynt, yrms = (S(2) for _ in range(6))
        E8 = S(8, DEC_B)
        mark_row = S(2)

        T = Carve(arena, tmp0, ARENA)
        hn = T(2, D_MODEL)
        sqj = T(2, D_MODEL)
        rope = T(2, TOK)
        xsw, rot1, rot2 = T(2, HALF), T(2, HALF), T(2, HALF)
        T = Carve(arena, tmp0, ARENA)
        vt, rgs, erg, ktok, sc = T(2, RET_W), T(2, RET_W), T(2, RET_W), T(2, RET_W), T(2, RET_W)
        ret_o, ret_c, ret_q = T(RET_W), T(RET_W), T(RET_W)
        qexp = T(H_RET, NSAMP * DEC_B)
        dtT = T(TOK)
        T = Carve(arena, tmp0, ARENA)
        S_ssm = T(8 * P_SSD)
        scv, cvo = T(NCT, 24), T(NCT, 27)
        xr = T(2, CONV_K - 1 + SEQ + DEC_B * (DEC_S + 3))
        cb_, ce = T(2, TOK), T(2, TOK)
        T = Carve(arena, tmp0 + 8 * P_SSD, ARENA)
        xs, xdt, wx, ud, wl = T(SSD_W), T(SSD_W), T(SSD_W), T(2, 4 * P), T(H_SSD * P)
        yb, ez, zs, btz = T(SSD_W), T(SSD_W), T(SSD_W), T(2, P)
        czexp = wl[:, 1024:2048]
        spo = zs[:, 0:512]
        yjunk, bexp = ez[:, 0:512], ez[:, 512:1024]
        dtx = ud.rearrange("p a b -> p (a b)")
        ge, mix2 = xs[:, 0:2 * HALF].rearrange("p (a b) -> p a b", a=2), xdt[:, 0:HALF]
        T = Carve(arena, tmp0, ARENA)
        lgT = T(NT * P)
        glog, elog = T(NT, N_GRP), T(NT, N_EXP)
        rt1, rt2, rt3 = (T(NT) for _ in range(3))
        gmax, gden, gidx, m1, m2, i1, i2, w1, w2 = (T(NT) for _ in range(9))
        r4a, r4b = T(NT, N_GRP), T(NT, N_GRP)
        ra, rb, oh1, oh2, rank, slot_e = (T(NT, N_EXP) for _ in range(6))
        hit = T(NT + 1, N_EXP)
        tot, otile, obase, oscan, oend = (T(N_EXP) for _ in range(5))
        slots_f = T(2, NT)
        ov_a, ov_b, ov_c = T(OVER, N_EXP), T(OVER, N_EXP), T(OVER)
        onT_at = (KD + KD + 3) * TOK
        T = Carve(arena, onT_at, tmp0)
        xn = T(NT, D_MODEL)
        tT = T(2, KD, P)
        T = Carve(arena, 0, onT_at)
        sq2 = T(D_MODEL)
        gf = T(D_MODEL)
        xrow = T(2, D_MODEL)
        xsT = T(2, KD, P)
        fe, fa, aT, fo = T(D_FF), T(2, D_FF), T(2, 4, P), T(2, D_MODEL)
        T = Carve(arena, D_MODEL, tmp0)
        got = T(2 * NT, D_MODEL)

        banks = []
        for i in range(8):
            ap = ctx.enter_context(nc.psum_tensor(f"psum{i}", [P, 512], F32))
            banks.append(Bank(ap[:, :], sem(f"psum{i}_full"), sem(f"psum{i}_free"), plan, i))
        bk = [b.ap for b in banks]

        slot_loaded = [sem(f"slot_loaded{i}") for i in range(RING)]
        slot_used = [sem(f"slot_used{i}") for i in range(RING)]
        engines_done, layer_cleared, aside = sem("engines_done"), sem("layer_cleared"), sem("aside")
        scattered = sem("scattered")
        gathered = [sem(f"gathered{i}") for i in range(2 * NT)]
        x_loaded = [sem(f"x_loaded{t}") for t in range(NT)]
        const_loaded, sums_zeroed, setup_made, zeroed, final_loaded, final_made, stored = (
            sem(n) for n in ("const_loaded", "sums_zeroed", "setup_made", "zeroed", "final_loaded", "final_made", "stored"))
        for n in plan.get("names", ()):
            signal(n)
        xrow_in = [sem(f"xrow_in{s}") for s in range(2)]
        out_stored = [sem(f"out_stored{s}") for s in range(2)]
        x_T, x_Tc, gate_up, sig_e, acted, act_T, act_Tc, down_ok, out_ok = (
            sem(n) for n in ("rows_turned", "rows_copied", "gate_up_done", "expo_done", "acted", "act_turned", "act_copied",
                             "down_done", "out_copied"))
        moe_chain = sem("moe_chain")
        LATE = ("slots", "dve_step", "rows_ready", "combined", "next_sq", "next_var", "next_ln", "next_rs")
        loop_sems = xrow_in + out_stored + [x_T, x_Tc, gate_up, sig_e, acted, act_T, act_Tc, down_ok, out_ok, moe_chain]

        block = ctx.enter_context(nc.Block())
        G = [float(v) for v in gammas()]

        def bc(ap, n):
            return ap.unsqueeze(len(ap.shape)).broadcast_to([*ap.shape, n])

        def bm(ap, n):
            return ap.unsqueeze(1).broadcast_to([ap.shape[0], n, *ap.shape[1:]])

        def ring_slot(name):
            n = UNIT_NO[name]
            return n % RING, n // RING

        def need_unit(pe, name):
            s, n = ring_slot(name)
            pe.wait_ge(slot_loaded[s], 16 * (n + 1))

        def unit_done(ins, name):
            ins.then_inc(slot_used[ring_slot(name)[0]], 1)

        def win(name):
            return ring[:, ring_slot(name)[0], :].rearrange("p (k n) -> p k n", k=KD)

        def meet(eng, L):
            eng.drain().then_inc(engines_done, 1)
            eng.wait_ge(layer_cleared, L + 1)
            eng.sem_inc(aside, 1)

        @block.sync
        def _(sp):
            for t in range(SAMPLE):
                sp.dma_start(X[:, t, :], x_p[0, t * P:(t + 1) * P, :]).then_inc(x_loaded[t], 16)
            sp.dma_start(X[0:NSAMP, SAMPLE, :], x_s.rearrange("b s d -> (b s) d")).then_inc(x_loaded[SAMPLE], 16)
            sp.dma_start(const[:], table[:, 0:CONST_COLS]).then_inc(const_loaded, 16)
            with sp.Fori(0, DEPTH) as L:
                for s in range(RING):
                    sp.sem_inc(slot_used[s], 1)

                def unit(name):
                    s, n = ring_slot(name)
                    sp.wait_ge(slot_used[s], n + 1)
                    _, col, w = UNITS[UNIT_NO[name]]
                    dst = ring[:, s, :]
                    if name[0:2] == "ro":
                        src = w_ret_out[L, :, col:col + w].rearrange("(k p) n -> p k n", p=P)
                        dst = dst[:, 0:RET_W // P * w].rearrange("p (k n) -> p k n", k=RET_W // P)
                    elif name[0:2] in ("so", "wo"):
                        m = w_ssd_out if name[0] == "s" else w_o
                        src = m[L, :, col:col + w].rearrange("(k p) n -> p k n", p=P)
                        dst = dst.rearrange("p (k n) -> p k n", k=KD)
                    else:
                        src = w_in[L, :, col:col + w].rearrange("(k p) n -> p k n", p=P)
                        dst = dst.rearrange("p (k n) -> p k n", k=KD)[:, :, 0:w]
                    sp.dma_start(dst, src).then_inc(slot_loaded[s], 16)

                with nc.allow_non_contiguous_dma(reason="small per-feature vectors"):
                    signal("g1").mark(sp.dma_start(g1, ln1_g[L].rearrange("(k p) -> p k", p=P)), "in", 16)
                    unit("q")
                    signal("rope").mark(sp.dma_start(rope.rearrange("p a t -> p (a t)"), table[:, CONST_COLS:]), "in", 16)
                    unit("k")
                    unit("v")
                    for dst, src in ((conv_bT, conv_b), (gnT, ret_gn_g), (sngT, ssd_norm_g), (g2, ln2_g)):
                        signal("vectors").mark(sp.dma_start(dst, src[L].rearrange("(k p) -> p k", p=P)), "in", 16)
                    for j in range(CONV_K):
                        signal("vectors").mark(sp.dma_start(conv_wT[:, :, j], conv_w[L, j].rearrange("(k p) -> p k", p=P)), "in", 16)
                    for dst, src in ((dskip, d_skip), (alog, a_log), (dtb, dt_bias)):
                        signal("head_vectors").mark(sp.dma_start(dst, src[L].partition_broadcast(P)), "in", 16)
                    signal("router_w").mark(sp.dma_start(w_router[:, :, 0:N_GRP], w_rg[L].rearrange("(k p) n -> p k n", p=P)), "in", 16)
                    signal("router_w").mark(sp.dma_start(w_router[:, :, N_GRP:], w_re[L].rearrange("(k p) n -> p k n", p=P)), "in", 16)
                for b in range(0, DEC_B, 2):
                    signal("natR").mark(sp.dma_start(natR[:, b:b + 2], state_ret[L, b:b + 2].rearrange("b h k v -> k b h v")), "in", 16)

                for t in range(SAMPLE):
                    sp.wait_ge(x_loaded[t], 16)
                sx = signal("x_spilled")
                sx.mark(sp.dma_start(x_spill[0:SEQ, :].rearrange("(t p) d -> p t d", p=P), X[:, 0:4, :]), "out", 16)

                unit("rg")
                signal("scv_nat").mark(sp.dma_start(cvn_in[0:24, :], state_conv[L].rearrange("b j c -> (b j) c")), "in", 16)
                signal("w_dt").mark(sp.dma_start(w_dt[:], w_in[L, :, COL_DT:COL_DT + H_SSD].rearrange("(k p) n -> p k n", p=P)), "in", 16)
                for name in ("x0", "x1", "x2"):
                    unit(name)
                banks[7].wait_freed(sp, ("kv", 3))
                signal("out_retp").mark(sp.dma_start(ret_p[L, 0].rearrange("h k v -> k h v"), S_ret.rearrange("p (h v) -> p h v", h=H_RET)), "out", 16)
                banks[7].wait_freed(sp, ("kvs", H_RET - 1, 0))
                banks[4].wait_freed(sp, ("kvs", H_RET - 1, 1))
                signal("out_rets").mark(sp.dma_start(ret_s[L].rearrange("b h k v -> k (b h) v"), nat.rearrange("p (c x) k -> p c (x k)", x=2)), "out", 16)
                signal("out_rets").wait(sp, "out")
                for c in range(8):
                    signal("natS").mark(sp.dma_start(natS[:, :, c % 4, c // 4, :], state_ssm[L, :, 2 * c:2 * c + 2].rearrange("b j p k -> (j p) b k")), "in", 16)
                unit("z0")
                unit("z1")
                for q in range(3):
                    banks[4 + q].wait_freed(sp, ("cvo", q))
                signal("out_convp").mark(sp.dma_start(conv_p[L, 0], cvo_n[0:3, :]), "out", 16)
                signal("out_convs").mark(sp.dma_start(conv_s[L].rearrange("b j c -> (b j) c"), cvo_n[3:27, :]), "out", 16)
                unit("gr0")
                banks[4].wait_freed(sp, ("spo",))
                for g in range(G_SSD):
                    signal("out_ssmp").mark(sp.dma_start(ssm_p[L, 0, 8 * g:8 * g + 8].rearrange("(c j) p k -> (j p) c k", j=2),
                                                         spo.rearrange("p (c g k) -> p c g k", g=2, k=64)[:, :, g, :]), "out", 16)
                unit("ro0")
                unit("gr1")
                banks[4].wait_freed(sp, ("bxs", 7))
                for c in range(8):
                    signal("out_ssms").mark(sp.dma_start(ssm_s[L, :, 2 * c:2 * c + 2].rearrange("b j p k -> (j p) b k"), natS[:, :, c % 4, c // 4, :]), "out", 16)
                for name in ("ro1", "gs0", "so0"):
                    unit(name)
                sx.wait(sp, "out")
                banks[6].wait(sp, ("yst", SAMPLE, 1))
                sx.mark(sp.dma_start(X[:, 0:4, :], x_spill[0:SEQ, :].rearrange("(t p) d -> p t d", p=P)), "in", 16)
                for name in ("gs1", "so1", "wo0", "wo1"):
                    unit(name)

                def load_rows(j, s, after):
                    if after is not None:
                        sp.wait_ge(x_T, after)
                    sp.dma_start(xrow[:, s, :], slot_in[bass.ds(j * P, P), :]).then_inc(xrow_in[s], 16)

                def load_expert(which, e_no, j):
                    sp.wait_ge(slot_used[MOE_SLOT[which]], j + (PHASE_USES[which] + 1))
                    m = (w_gate, w_up, w_down)[which]
                    sp.dma_start(ring[:, MOE_SLOT[which], :].rearrange("p (k n) -> p k n", k=(KD, KD, D_FF // P)[which]),
                                 m[L, e_no].rearrange("(k p) n -> p k n", p=P)).then_inc(slot_loaded[MOE_SLOT[which]], 16)

                for key in ("retp", "rets", "convp", "convs", "ssmp", "ssms"):
                    signal("out_" + key).wait(sp, "out")

                def load_tiles(first, count, expert):
                    def pair(j, e):
                        load_expert(0, e, j)
                        load_expert(1, e, j)

                    pair(first, expert(first))
                    signal("rows_ready").wait(sp, "all")
                    load_rows(first, 0, first - 1 if first else None)
                    load_rows(first + 1, 1, first if first else None)
                    if first == 0:
                        with sp.Fori(0, (count - 2) // 2) as t2:
                            for s in range(2):
                                j = t2 * 2 + (first + s)
                                pair(j + 1, j + 1)
                                load_rows(j + 2, s, j + 1)
                                load_expert(2, j, j)
                        peeled = range(first + count - 2, first + count)
                    else:
                        peeled = range(first, first + count)
                    for j in peeled:
                        if j + 1 < first + count:
                            pair(j + 1, expert(j + 1))
                        if j + 2 < first + count:
                            load_rows(j + 2, j % 2, j + 1)
                        load_expert(2, expert(j), j)

                load_tiles(0, MAIN, lambda j: j)
                sp.wait_ge(x_T, 1)
                sp.wait_ge(x_Tc, 2)
                sp.wait_ge(act_Tc, 1)
                late = [signal(n).sem for n in LATE]
                for s in [x.sem for x in signals.values() if x.sem not in late] + [b.full for b in banks] + [b.free for b in banks]:
                    sp.sem_clear(s)
                n_extra = sp.value_load(over_i[0:1, OVER:OVER + 1], min_val=0, max_val=OVER)
                with sp.If(n_extra > 0):
                    e_of = {}

                    def named(j):
                        if j not in e_of:
                            e_of[j] = sp.value_load(over_i[0:1, j - MAIN:j - MAIN + 1], min_val=0, max_val=N_EXP - 1)
                        return e_of[j]

                    load_tiles(MAIN, OVER, named)

                sp.wait_ge(engines_done, L * 4 + 4)
                sp.sem_inc(aside, 1)
                for s in late + loop_sems + slot_loaded + slot_used:
                    sp.sem_clear(s)
                sp.sem_inc(layer_cleared, 1)
            sp.dma_start(gf, lnf_g.partition_broadcast(P)).then_inc(final_loaded, 16)
            sp.wait_ge(final_made, 1)
            sp.dma_start(y_p.rearrange("b (t p) d -> p (b t) d", p=P), xn[:, 0:4, :]).then_inc(stored, 16)
            sp.dma_start(y_s.rearrange("b s d -> (b s) d"), xn[0:NSAMP, SAMPLE, :]).then_inc(stored, 16)
            sp.wait_ge(stored, 32)

        @block.tensor
        def _(pe):
            W = nc.tensor
            pe.wait_ge(const_loaded, 16)
            pe.wait_ge(setup_made, 1)

            def turn(bank, key, srcs, wait=None, width=P):
                b = banks[bank]
                b.acquire(pe, key)
                if wait:
                    signal(wait[0]).wait(pe, wait[1])
                for i, src in enumerate(srcs):
                    n, m = src.shape[0], int(np.prod(src.shape[1:]))
                    last = W.transpose(b.ap[0:m, i * width:i * width + n], src, C("ident", n)[:, 0:n])
                b.filled(last)

            def fmajor(name, cc, half, bank, key, lhs_k=KD, rhs=None, last_of=False):
                rhs = hT if rhs is None else rhs
                w = ring[:, ring_slot(name)[0], 0:lhs_k * UNIT].rearrange("p (k n) -> p k n", k=lhs_k)
                b = banks[bank]
                b.acquire(pe, key)
                for k in range(lhs_k):
                    last = W.matmul(b.ap[:, 0:HALF], w[:, k, cc * P:cc * P + P], rhs[:, k, half * HALF:(half + 1) * HALF],
                                    start=(k == 0), stop=(k == lhs_k - 1))
                b.filled(last)
                return last

            def tmajor(name, t, bank, key, src=None):
                src = hT if src is None else src
                b = banks[bank]
                b.acquire(pe, key)
                for k in range(KD):
                    last = W.matmul(b.ap[0:rows(t), :], src[:, k, tok(t)], win(name)[:, k, :], start=(k == 0), stop=(k == KD - 1))
                b.filled(last)

            def done(name):
                W.drain().then_inc(slot_used[ring_slot(name)[0]], 1)

            with pe.Fori(0, DEPTH) as L:
                for t in range(NT):
                    for h in range(2):
                        turn(2 + h, ("hT", t, h), [hn[0:rows(t), t % 2, (4 * h + i) * P:(4 * h + i + 1) * P] for i in range(4)],
                             ("hn", t))
                g = 0
                for u, name in enumerate(("q", "k")):
                    need_unit(pe, name)
                    for cc in range(4):
                        for half in range(2):
                            for h in range(2):
                                banks[2 + h].wait_freed(pe, ("hT", NT - 1 if half else 2, h))
                            fmajor(name, cc, half, g % 2, ("qk", g))
                            g += 1
                    done(name)
                need_unit(pe, "v")
                need_unit(pe, "rg")
                for t in range(NT):
                    n = rows(t)
                    turn(2, ("ktok", t), [qk[:, 4 + h, tok(t)] for h in range(H_RET)], ("qk", 15 if t >= 2 else 14))
                    b = banks[4]
                    b.acquire(pe, ("scores", t))
                    for h in range(H_RET):
                        last = W.matmul(b.ap[0:n, h * n:(h + 1) * n], qk[:, 4 + h, tok(t)], qk[:, h, tok(t)], start=True, stop=True)
                    b.filled(last)
                    tmajor("v", t, 0, ("v", t))
                    tmajor("rg", t, 1, ("rg", t))
                    if t == SAMPLE:
                        done("v")
                        done("rg")
                    banks[4].wait_freed(pe, ("scores", t))
                    banks[0].wait_freed(pe, ("v", t))
                    b = banks[5]
                    b.acquire(pe, ("intra", t))
                    for h in range(H_RET):
                        last = W.matmul(b.ap[0:n, h * DV:(h + 1) * DV], sc[0:n, t % 2, h * n:(h + 1) * n],
                                        vt[0:n, t % 2, h * DV:(h + 1) * DV], start=True, stop=True)
                    b.filled(last)
                    b = banks[6]
                    b.acquire(pe, ("inter", t))
                    if t < SAMPLE:
                        signal("state_zero").wait(pe, "ret")
                        if t:
                            banks[7].wait_freed(pe, ("kv", t - 1))
                        for h in range(H_RET):
                            last = W.matmul(b.ap[:, h * DV:(h + 1) * DV], qk[:, h, tok(t)], S_ret[:, h * DV:(h + 1) * DV], start=True, stop=True)
                    else:
                        signal("natR").wait(pe, "in")
                        for h in range(H_RET):
                            signal("qexp").wait(pe, h)
                            for q in range(DEC_B):
                                last = W.matmul(b.ap[0:n, h * DV:(h + 1) * DV], qexp[:, h, q * NSAMP:(q + 1) * NSAMP], natR[:, q, h, :],
                                                start=(q == 0), stop=(q == DEC_B - 1))
                    b.filled(last)
                    banks[2].wait_freed(pe, ("ktok", t))
                    if t < SAMPLE:
                        b = banks[7]
                        b.acquire(pe, ("kv", t))
                        for h in range(H_RET):
                            last = W.matmul(b.ap[:, h * DV:(h + 1) * DV], ktok[:, t % 2, h * DV:(h + 1) * DV], vt[:, t % 2, h * DV:(h + 1) * DV],
                                            start=True, stop=True)
                        b.filled(last)
                    else:
                        for h in range(H_RET):
                            for q in range(2):
                                signal("vexp").wait(pe, (h, q))
                                b = banks[(7, 4)[q]]
                                b.acquire(pe, ("kvs", h, q))
                                last = W.matmul(b.ap[:, :], ktok[0:n, t % 2, h * DV:(h + 1) * DV],
                                                vexp[0:n, 4 * q:4 * q + 4, :].rearrange("p b v -> p (b v)"), start=True, stop=True)
                                b.filled(last)
                    if t >= 1:
                        turn(3, ("onT", t - 1), [ret_q[0:rows(t - 1), i * P:(i + 1) * P] for i in range(4)], ("gated", t - 1))
                signal("w_dt").wait(pe, "in")
                for half in range(2):
                    b = banks[5 - half]
                    b.acquire(pe, ("dtT", half))
                    for k in range(KD):
                        last = W.matmul(b.ap[0:H_SSD, 0:HALF], w_dt[:, k, :], hT[:, k, half * HALF:(half + 1) * HALF], start=(k == 0), stop=(k == KD - 1))
                    b.filled(last)
                turn(3, ("onT", SAMPLE), [ret_q[0:NSAMP, i * P:(i + 1) * P] for i in range(4)], ("gated", SAMPLE))
                turn(2, ("scv",), [cvn_in[0:24, i * P:(i + 1) * P] for i in range(NCT)], ("scv_nat", "in"), width=24)
                g = 0
                for name, n_cc in (("x0", 4), ("x1", 4), ("x2", 2)):
                    need_unit(pe, name)
                    for cc in range(n_cc):
                        for half in range(2):
                            fmajor(name, cc, half, half, ("x", g, half))
                        if g == 0:
                            b = banks[3]
                            b.acquire(pe, ("dt",))
                            for half in range(2):
                                banks[5 - half].wait_freed(pe, ("dtT", half))
                            for t in range(NT):
                                last = W.transpose(b.ap[0:rows(t), t * H_SSD:(t + 1) * H_SSD], dtT[0:H_SSD, tok(t)], C("ident", H_SSD)[:, 0:H_SSD])
                            b.filled(last)
                        g += 1
                    done(name)
                    if name == "x1":
                        b = banks[3]
                        b.acquire(pe, ("cum",))
                        signal("dta").wait(pe, 0)
                        for t in range(NT):
                            n = rows(t)
                            for q, m in enumerate((("upto", "ones") if t < SAMPLE else ("upto_s", "ones_s"))):
                                last = W.matmul(b.ap[0:n, t * 32 + 16 * q:t * 32 + 16 * q + 16], C(m, n)[:, 0:n], dta[0:n, t, :], start=True, stop=True)
                        b.filled(last)
                for q, (a, z) in enumerate(((0, 4), (4, 8), (8, 10))):
                    turn(4 + q, ("cvo", q), [cvo[:, i, :] for i in range(a, z)], ("cvo", NCT - 1))
                need_unit(pe, "z0")
                need_unit(pe, "z1")
                tmajor("z0", 0, 0, ("z", 0, 0))
                tmajor("z1", 0, 1, ("z", 0, 1))
                for t in range(NT):
                    n = rows(t)
                    if t == SAMPLE:
                        for r in range(8):
                            turn(2 + r % 2, ("ssmT", r), [natS[:, r, h, :, :].rearrange("p g k -> p (g k)") for h in range(4)],
                                 ("natS", "in"))
                    for h in range(2):
                        if t == 0:
                            signal("conv").wait(pe, 4 * h + 3)
                        turn(2 + h, ("xsT", t, h), [conv[:, 4 * h + i, tok(t)] for i in range(4)])
                    b = banks[4]
                    b.acquire(pe, ("cb", t))
                    if t == 0:
                        signal("conv").wait(pe, NCT - 1)
                    W.matmul(b.ap[0:n, 0:2 * n], conv[:, 8, tok(t)], conv[:, 9:11, tok(t)], start=True, stop=True)
                    b.filled(W.transpose(b.ap[0:n, 256:384], conv[:, 8, tok(t)], C("ident")))
                    for r in range(4):
                        if t and r == 2:
                            tmajor("z1", t, 1, ("z", t, 1))
                            if t == SAMPLE:
                                done("z1")
                        b = banks[5 + r % 2]
                        b.acquire(pe, ("seg", t, r))
                        mask = neg[0:n, 0:P] if t < SAMPLE else neg[0:n, P:P + NSAMP]
                        for h in range(4):
                            W.matmul(b.ap[0:n, h * n:(h + 1) * n], ident16[0:n, 0:n], mask, start=(h == 0), stop=False, skip_group_check=True)
                        signal("ud").wait(pe, (t, r))
                        last = W.matmul(b.ap[0:n, 0:4 * n], C("ones", n)[:, 0:n], ud[0:n, r % 2, 0:4 * n], start=False, stop=True, skip_group_check=True)
                        b.filled(last)
                    if t >= 1:
                        for h in range(2):
                            turn(2 + h, ("yT", t - 1, h), [yb[0:rows(t - 1), (4 * h + i) * P:(4 * h + i + 1) * P] for i in range(4)], ("y", t - 1))
                    banks[4].wait_freed(pe, ("cb", t))
                    for h in range(2):
                        banks[2 + h].wait_freed(pe, ("xsT", t, h))
                    for g in range(2):
                        b = banks[2 + g]
                        b.acquire(pe, ("yin", t, g))
                        for h in range(8):
                            hh = 8 * g + h
                            last = W.matmul(b.ap[0:n, h * 64:(h + 1) * 64], wl[0:n, hh * n:(hh + 1) * n], xdt[0:n, hh * 64:(hh + 1) * 64], start=True, stop=True)
                        b.filled(last)
                    if t < SAMPLE:
                        signal("state_zero").wait(pe, "ssm")
                        if t:
                            banks[7].wait_freed(pe, ("bx", t - 1))
                    for g in range(2):
                        b = banks[5 + g]
                        b.acquire(pe, ("yst", t, g))
                        if t < SAMPLE:
                            last = W.matmul(b.ap[:, :], conv[:, 9 + g, tok(t)], S_ssm, start=True, stop=True)
                        else:
                            for r in (6, 7):
                                banks[2 + r % 2].wait_freed(pe, ("ssmT", r))
                            signal("czexp").wait(pe, g)
                            for q in range(DEC_B):
                                last = W.matmul(b.ap[0:n, :], czexp[:, g * 512 + q * 64:g * 512 + (q + 1) * 64], ssmT[:, q, :], start=(q == 0), stop=(q == DEC_B - 1))
                        b.filled(last)
                    signal("btz").wait(pe, t)
                    signal("wx").wait(pe, t)
                    if t < SAMPLE:
                        b = banks[7]
                        b.acquire(pe, ("bx", t))
                        for g in range(2):
                            last = W.matmul(b.ap[:, :], btz[:, g, :], wx[:, g * 512:(g + 1) * 512], start=(g == 0), stop=(g == 1))
                        b.filled(last)
                    else:
                        b = banks[7]
                        b.acquire(pe, ("e8",))
                        signal("dtx").wait(pe, 0)
                        for c in range(8):
                            last = W.matmul(b.ap[:, c * 8:(c + 1) * 8], dtx[0:n, c * P:(c + 1) * P], C("seqcol", n), start=True, stop=True)
                        b.filled(last)
                        for c in range(8):
                            b = banks[(7, 4)[c % 2]]
                            b.acquire(pe, ("bxs", c))
                            signal("bexp").wait(pe, c // 4)
                            last = W.matmul(b.ap[:, :], wx[0:n, c * P:(c + 1) * P], bexp[0:n, :], start=True, stop=True)
                            b.filled(last)
                    if t < SAMPLE:
                        tmajor("z0", t + 1, 0, ("z", t + 1, 0))
                        if t + 1 == SAMPLE:
                            done("z0")
                    if t == SAMPLE - 1:
                        banks[7].wait_freed(pe, ("bx", t))
                        turn(4, ("spo",), [S_ssm[:, i * P:(i + 1) * P] for i in range(4)])
                def gate(g):
                    br, c, half = g // 16, g // 2 % 8, g % 2
                    name = ("gr", "gs")[br] + str(c // 4)
                    if c % 4 == 0 and half == 0:
                        need_unit(pe, name)
                    fmajor(name, c % 4, half, g % 2, ("gate", g))
                    if c % 4 == 3 and half == 1:
                        done(name)

                def branch(g):
                    br, c, half = g // 16, g // 2 % 8, g % 2
                    name = ("ro", "so")[br] + str(c // 4)
                    if c % 4 == 0 and half == 0:
                        need_unit(pe, name)
                    if g == 0:
                        banks[3].wait_freed(pe, ("onT", SAMPLE))
                    if g == 16:
                        for h in range(2):
                            banks[5 + h].wait_freed(pe, ("yT", SAMPLE, h))
                    fmajor(name, c % 4, half, 2 + g % 2, ("branch", g), lhs_k=(RET_W // P, KD)[br], rhs=(onT, yT)[br])
                    if c % 4 == 3 and half == 1:
                        done(name)

                gate(0)
                for g in range(32):
                    if g < 31:
                        gate(g + 1)
                    branch(g)
                    if g == 0:
                        for h in range(2):
                            turn(5 + h, ("yT", SAMPLE, h), [yb[0:NSAMP, (4 * h + i) * P:(4 * h + i + 1) * P] for i in range(4)], ("y", SAMPLE))
                need_unit(pe, "wo0")
                need_unit(pe, "wo1")
                signal("mix").wait(pe, 31)

                def turn_xn(t):
                    for h in range(2):
                        turn(2 + h, ("tT", t, h), [xn[0:rows(t), t, (4 * h + i) * P:(4 * h + i + 1) * P] for i in range(4)], ("xn", t))

                def route(t):
                    b = banks[0]
                    b.acquire(pe, ("logits", t))
                    for h in range(2):
                        banks[2 + h].wait_freed(pe, ("tT", t, h))
                    for k in range(KD):
                        last = W.matmul(b.ap[0:N_GRP + N_EXP, 0:rows(t)], w_router[:, k, :], tT[:, t % 2, k, 0:rows(t)],
                                        start=(k == 0), stop=(k == KD - 1))
                    b.filled(last)

                signal("router_w").wait(pe, "in")
                for t in range(NT):
                    tmajor("wo0", t, 4 + (2 * t) % 4, ("wo", t, 0), src=mT)
                    if t:
                        turn_xn(t - 1)
                    tmajor("wo1", t, 4 + (2 * t + 1) % 4, ("wo", t, 1), src=mT)
                    if t:
                        route(t - 1)
                done("wo0")
                done("wo1")
                turn_xn(SAMPLE)
                route(SAMPLE)
                b = banks[1]
                b.acquire(pe, ("router",))
                for t in range(NT):
                    banks[0].wait_freed(pe, ("logits", t))
                    last = W.transpose(b.ap[0:rows(t), t * 20:t * 20 + 20], lgT[0:20, t * P:t * P + rows(t)], C("ident", 20)[:, 0:20])
                b.filled(last)
                signal("hit").wait(pe, 0)
                b = banks[0]
                b.acquire(pe, ("rank",))
                flat = hit.rearrange("p t e -> p (t e)")
                W.matmul(b.ap[:, 0:(NT + 1) * N_EXP], C("before"), flat, start=True, stop=False, skip_group_check=True)
                for d in range(1, NT + 1):
                    last = W.matmul(b.ap[:, d * N_EXP:(NT + 1) * N_EXP], C("ones"), flat[:, 0:(NT + 1 - d) * N_EXP],
                                    start=False, stop=(d == NT), skip_group_check=True)
                b.filled(last)

                for b in banks:
                    if b.releases():
                        pe.wait_ge(b.free, b.releases())

                def weights(which, j):
                    pe.wait_ge(slot_loaded[MOE_SLOT[which]], j * 16 + 16 * (PHASE_USES[which] + 1))

                def turn_rows(s, j, half_j):
                    pe.wait_ge(xrow_in[s], half_j * 16 + 16)
                    if not isinstance(j, int) or j > 1:
                        pe.wait_ge(act_Tc, j - 1)
                    elif j == 1:
                        pe.wait_ge(x_Tc, 1)
                    for i in range(KD):
                        last = W.transpose(bk[2 + i // 4][:, (i % 4) * P:(i % 4 + 1) * P], xrow[:, s, i * P:(i + 1) * P], C("ident"))
                    last.then_inc(x_T, 1)

                def gate_up_mm(s, j):
                    pe.wait_ge(x_Tc, j + 1)
                    if not isinstance(j, int) or j > 0:
                        pe.wait_ge(acted, j)
                    for which in range(2):
                        weights(which, j)
                        w = ring[:, MOE_SLOT[which], :].rearrange("p (k n) -> p k n", k=KD)
                        for k in range(KD):
                            last = W.matmul(bk[which], xsT[:, s, k, :], w[:, k, :], start=(k == 0), stop=(k == KD - 1))
                        if which == 0:
                            last.then_inc(slot_used[MOE_SLOT[0]], 1)
                    last.then_inc(gate_up, 1)
                    W.drain().then_inc(slot_used[MOE_SLOT[1]], 1)

                def down_mm(s, j):
                    pe.wait_ge(act_Tc, j + 1)
                    pe.wait_ge(out_ok, j + 1)
                    weights(2, j)
                    w = ring[:, MOE_SLOT[2], :].rearrange("p (k n) -> p k n", k=4)
                    for h in range(2):
                        for k in range(4):
                            last = W.matmul(bk[4 + 2 * s + h], aT[:, s, k, :], w[:, k, h * 512:(h + 1) * 512], start=(k == 0), stop=(k == 3))
                    last.then_inc(down_ok, 1)
                    W.drain().then_inc(slot_used[MOE_SLOT[2]], 1)

                def turn_act(s, j, more=True):
                    pe.wait_ge(acted, j + 1)
                    if more:
                        pe.wait_ge(x_Tc, j + 2)
                    for i in range(4):
                        last = W.transpose(bk[2][:, i * P:(i + 1) * P], fa[:, s, i * P:(i + 1) * P], C("ident"))
                    last.then_inc(act_T, 1)

                def multiply_tiles(first, count):
                    last = first + count - 1
                    turn_rows(0, first, first // 2)
                    gate_up_mm(0, first)
                    turn_rows(1, first + 1, first // 2)
                    turn_act(0, first)
                    with pe.Fori(0, (count - 2) // 2) as t2:
                        for q in range(2):
                            s, j = 1 - q, t2 * 2 + (first + 1 + q)
                            gate_up_mm(s, j)
                            turn_rows(1 - s, j + 1, t2 + (first // 2 + 1))
                            down_mm(1 - s, j - 1)
                            turn_act(s, j)
                    gate_up_mm(1, last)
                    down_mm(0, last - 1)
                    turn_act(1, last, more=False)
                    down_mm(1, last)

                multiply_tiles(0, MAIN)
                signal("slots").wait(pe, "over")
                with pe.If(pe.value_load(over_i[0:1, OVER:OVER + 1], min_val=0, max_val=OVER) > 0):
                    multiply_tiles(MAIN, OVER)
                meet(pe, L)

        class Chain:

            def __init__(self, eng, name):
                self.eng, self.sig, self.n = eng, signal(name), 0

            def __call__(self, ins):
                self.n += 1
                self.sig.mark(ins, self.n)
                self.sig.wait(self.eng, self.n)

        @block.scalar
        def _(act):
            a = nc.scalar

            def input_sums(name, ready):
                for t in range(NT):
                    ready(t)
                    if t >= 2:
                        signal(name + "_sq").wait(act, t - 2)
                    signal(name + "_sq").mark(a.activation(sqj[0:rows(t), t % 2, :], X[0:rows(t), t, :], ACT.Square, accum_out=ssq[0:rows(t), t:t + 1]), t)
                signal(name + "_var").wait(act, 0)
                signal(name + "_ln").mark(a.activation(nln, nvar, ACT.Ln), 0)
                signal(name + "_ln").wait(act, 0)
                signal(name + "_rs").mark(a.activation(nrs, nln, ACT.Exp, scale=-0.5), 0)

            act.wait_ge(sums_zeroed, 1)
            input_sums("first", lambda t: act.wait_ge(x_loaded[t], 16))
            with act.Fori(0, DEPTH) as L:
                step = Chain(act, "act_step")

                def rsq(key, p, v, ln, rs):
                    signal("var").wait(act, key)
                    step(a.activation(ln[0:p], v[0:p], ACT.Ln))
                    signal("rs0").mark(a.activation(rs[0:p], ln[0:p], ACT.Exp, scale=-0.5), key)

                for g in range(16):
                    banks[g % 2].wait(act, ("qk", g))
                    if g >= 2:
                        banks[g % 2].wait_freed(act, ("qk", g - 2))
                    a.copy(xsw[0:64, g % 2, :], bk[g % 2][64:128, 0:HALF])
                    signal("xsw").mark(a.copy(xsw[64:128, g % 2, :], bk[g % 2][0:64, 0:HALF]), g)
                signal("qk").wait(act, 15)
                for t in range(NT):
                    n = rows(t)
                    banks[0].wait(act, ("v", t))
                    if t >= 2:
                        banks[5].wait(act, ("intra", t - 2))
                        banks[7].wait(act, ("kv", t - 2))
                    banks[0].release(a.copy(vt[0:n, t % 2, :], bk[0][0:n, :]), ("v", t))
                    banks[1].wait(act, ("rg", t))
                    if t >= 2:
                        banks[1].wait_freed(act, ("rg", t - 2))
                    signal("erg").mark(a.activation(erg[0:n, t % 2, :], bk[1][0:n, :], ACT.Exp, scale=-1.0), t)
                    rsq(("gn", t), n, gvar, gln, grs)
                signal("gated").wait(act, SAMPLE)
                for half in range(2):
                    b = banks[5 - half]
                    b.wait(act, ("dtT", half))
                    b.release(a.copy(dtT[0:H_SSD, half * HALF:(half + 1) * HALF], b.ap[0:H_SSD, 0:HALF]), ("dtT", half))
                banks[2].wait(act, ("scv",))
                banks[2].release(a.copy(scv.rearrange("p c r -> p (c r)"), bk[2][:, 0:24 * NCT]), ("scv",))
                banks[2].wait_freed(act, ("scv",))
                for g in range(NCT + 1):
                    if g < NCT:
                        pad = xr[:, g % 2, CONV_K - 1 + SEQ:].rearrange("p (b r) -> p b r", b=DEC_B)
                        if g >= 2:
                            signal("lin").wait(act, g - 2)
                            signal("cvo").wait(act, g - 2)
                        a.copy(pad[:, :, 0:3], scv[:, g, :].rearrange("p (b r) -> p b r", b=DEC_B))
                        banks[0].wait(act, ("x", g, 0))
                        banks[0].release(a.copy(xr[:, g % 2, 3:3 + HALF], bk[0][:, 0:HALF]), ("x", g, 0))
                        banks[1].wait(act, ("x", g, 1))
                        a.copy(xr[:, g % 2, 3 + HALF:3 + SEQ], bk[1][:, 0:HPRE])
                        banks[1].release(a.copy(pad[:, :, 3:], bk[1][:, HPRE:HALF].rearrange("p (b r) -> p b r", b=DEC_B)), ("x", g, 1))
                    if g >= 1:
                        signal("lin").wait(act, g - 1)
                        if g >= 3:
                            signal("conv").wait(act, g - 3)
                        signal("ce").mark(a.activation(ce[:, (g - 1) % 2, :], cb_[:, (g - 1) % 2, :], ACT.Exp, scale=-1.0), g - 1)
                    if g == 3:
                        signal("head_vectors").wait(act, "in")
                        signal("acoef").mark(a.activation(acoef, alog, ACT.Exp), 0)
                        signal("sp").wait(act, "arg")
                        signal("spa").mark(a.activation(dt2, dt1, ACT.Exp), "e")
                    if g == 5:
                        signal("sp").wait(act, "u")
                        signal("spa").mark(a.activation(dt3, dt1, ACT.Ln), "ln")
                    if g == NCT:
                        signal("decays").wait(act, "args")
                        a.activation(ecum, cum, ACT.Exp)
                        a.activation(dec, cend, ACT.Exp)
                        signal("decayed").mark(a.activation(wend, wend, ACT.Exp), 0)
                for q in range(3):
                    w = (CONV_DIM - 512 * q) if q == 2 else 512
                    banks[4 + q].wait(act, ("cvo", q))
                    banks[4 + q].release(a.copy(cvo_n[0:27, 512 * q:512 * q + w], bk[4 + q][0:27, 0:w]), ("cvo", q))
                signal("conv").wait(act, NCT - 1)
                for t in range(NT):
                    n = rows(t)
                    if t == SAMPLE:
                        signal("x_spilled").wait(act, "out")
                        for r in range(8):
                            b = banks[2 + r % 2]
                            b.wait(act, ("ssmT", r))
                            b.release(a.copy(ssmT[:, r, :], b.ap), ("ssmT", r))
                    for h in range(2):
                        b = banks[2 + h]
                        b.wait(act, ("xsT", t, h))
                        if t:
                            signal("ylin").wait(act, t - 1)
                        signal("xs").mark(a.copy(xs[0:n, 512 * h:512 * h + 512], b.ap[0:n, :]), (t, h))
                    if t:
                        banks[3].wait(act, ("yin", t - 1, 1))

                    def segs(r):
                        b = banks[5 + r % 2]
                        b.wait(act, ("seg", t, r))
                        for h in range(4):
                            hh = 4 * r + h
                            last = a.activation(wl[0:n, hh * n:(hh + 1) * n], b.ap[0:n, h * n:(h + 1) * n], ACT.Exp, bias=ncum[0:n, t, hh:hh + 1])
                        b.release(last, ("seg", t, r))

                    for r in range(4):
                        segs(r)
                    for h in range(2):
                        banks[h].wait(act, ("z", t, h))
                        if t:
                            banks[h].wait_freed(act, ("z", t - 1, h))
                        signal("ez").mark(a.activation(ez[0:n, 512 * h:512 * h + 512], bk[h][0:n, :], ACT.Exp, scale=-1.0), (t, h))
                    if t == SAMPLE:
                        banks[7].wait(act, ("e8",))
                        banks[7].release(a.activation(E8.rearrange("p c b -> p (c b)"), bk[7][:, 0:64], ACT.Exp), ("e8",))
                    signal("yz").wait(act, t)
                    if t == SAMPLE - 1:
                        banks[4].wait(act, ("spo",))
                        banks[4].release(a.copy(spo, bk[4]), ("spo",))
                    for g in range(2):
                        if g:
                            step(last)
                        last = a.activation(yjunk[0:n], yb[0:n, 512 * g:512 * g + 512], ACT.Square, accum_out=ysum[0:n, g:g + 1])
                    signal("ysq").mark(last, t)
                    rsq(("y", t), n, yvar, yln, yrs)
                signal("ylin").wait(act, SAMPLE)
                for g in range(32):
                    banks[g % 2].wait(act, ("gate", g))
                    if g >= 2:
                        banks[2 + g % 2].wait_freed(act, ("branch", g - 2))
                    banks[g % 2].release(a.activation(ge[:, g % 2, :], bk[g % 2][:, 0:HALF], ACT.Exp, scale=-1.0), ("gate", g))
                def copy_logits(t):
                    banks[0].wait(act, ("logits", t))
                    banks[0].release(a.copy(lgT[0:20, t * P:t * P + rows(t)], bk[0][0:20, 0:rows(t)]), ("logits", t))

                for t in range(NT):
                    for h in range(2):
                        banks[4 + (2 * t + h) % 4].wait_freed(act, ("wo", t, h))
                    if t:
                        signal("sq2").wait(act, t - 1)
                    signal("sq2").mark(a.activation(sq2[0:rows(t)], X[0:rows(t), t, :], ACT.Square, accum_out=ssq2[0:rows(t), t:t + 1]), t)
                    rsq(("n2", t), rows(t), nvar2[:, t:t + 1], nln2[:, t:t + 1], nrs2[:, t:t + 1])
                    if t:
                        copy_logits(t - 1)
                copy_logits(SAMPLE)
                signal("route").wait(act, "gd")
                signal("routea").mark(a.activation(r4b, r4a, ACT.Exp), "g")
                signal("route").wait(act, "ed")
                signal("routea").mark(a.activation(rt2, rt1, ACT.Exp), "e")
                act.sem_inc(out_ok, 2)
                for s in range(2):
                    act.sem_inc(out_stored[s], 16)

                def expo(j):
                    act.wait_ge(gate_up, j + 1)
                    if not isinstance(j, int) or j:
                        act.wait_ge(acted, j)
                    a.activation(fe, bk[0], ACT.Exp, scale=-1.0).then_inc(sig_e, 1)

                def copy_act(s, j):
                    act.wait_ge(act_T, j + 1)
                    if not isinstance(j, int) or j > 1:
                        act.wait_ge(down_ok, j - 1)
                    a.copy(aT[:, s, :, :].rearrange("p k n -> p (k n)"), bk[2]).then_inc(act_Tc, 1)

                def store(s, j, nth):
                    act.wait_ge(down_ok, j + 1)
                    act.wait_ge(out_stored[s], nth * 16 + 16)
                    for h in range(2):
                        last = a.copy(fo[:, s, h * 512:(h + 1) * 512], bk[4 + 2 * s + h])
                    last.then_inc(out_ok, 1)
                    act.wait_ge(out_ok, j + 3)
                    act.dma_start(slot_out[bass.ds(j * P, P), :], fo[:, s, :]).then_inc(out_stored[s], 16)

                def finish_tiles(first, count):
                    last = first + count - 1
                    expo(first)
                    copy_act(0, first)
                    with act.Fori(0, (count - 2) // 2) as t2:
                        for q in range(2):
                            s, j = 1 - q, t2 * 2 + (first + 1 + q)
                            expo(j)
                            store(1 - s, j - 1, t2 + first // 2)
                            copy_act(s, j)
                    expo(last)
                    store(0, last - 1, last // 2)
                    copy_act(1, last)
                    store(1, last, last // 2)

                finish_tiles(0, MAIN)
                signal("slots").wait(act, "over")
                with act.If(act.value_load(over_i[0:1, OVER:OVER + 1], min_val=0, max_val=OVER) > 0):
                    finish_tiles(MAIN, OVER)
                input_sums("next", lambda t: signal("combined").wait(act, t))
                meet(act, L)

        @block.vector
        def _(dve):
            v = nc.vector
            tt, ts, stt, cp = v.tensor_tensor, v.tensor_scalar, v.scalar_tensor_tensor, v.tensor_copy
            for ap in (zero[:], dts, cum, cend):
                v.memset(ap, 0.0)
            v.memset(ssq2, float(D_MODEL))
            v.memset(ssq, float(D_MODEL)).then_inc(sums_zeroed, 1)
            dve.wait_ge(sums_zeroed, 1)

            def input_rms(name, step):
                signal(name + "_sq").wait(dve, NT - 1)
                signal(name + "_var").mark(ts(nvar, ssq, 1.0 / D_MODEL, EPS, ALU.mult, ALU.add), 0)
                signal(name + "_var").wait(dve, 0)
                signal(name + "_rs").wait(dve, 0)
                step(tt(nnt, nvar, nrs, ALU.mult))
                step(tt(nnt, nnt, nrs, ALU.mult))
                step(ts(nnt, nnt, -0.5, 1.5, ALU.mult, ALU.add))
                step(tt(nrms, nnt, nrs, ALU.mult))

            dve.wait_ge(const_loaded, 16)
            first = Chain(dve, "dve_first")
            first(ts(neg[:, 0:P], C("upto"), 1.0, BIG, ALU.subtract, ALU.mult))
            first(ts(neg[:, P:P + NSAMP], C("upto_s"), 1.0, BIG, ALU.subtract, ALU.mult))
            cp(ident16[:], C("ident")).then_inc(setup_made, 1)
            input_rms("first", first)

            with dve.Fori(0, DEPTH) as L:
                step = Chain(dve, "dve_step")

                def refine(key, p, va, rs, nt, out):
                    signal("rs0").wait(dve, key)
                    step(tt(nt[0:p], va[0:p], rs[0:p], ALU.mult))
                    step(tt(nt[0:p], nt[0:p], rs[0:p], ALU.mult))
                    step(ts(nt[0:p], nt[0:p], -0.5, 1.5, ALU.mult, ALU.add))
                    step(tt(out[0:p], nt[0:p], rs[0:p], ALU.mult))

                def heads(ap, h, w):
                    return ap.rearrange("p (h w) -> p h w", h=h)

                signal("state_zero").mark(v.memset(S_ret, 0.0), "ret")
                signal("state_zero").wait(dve, "ret")
                signal("g1").wait(dve, "in")
                for t in range(NT + 1):
                    if t < NT:
                        n = rows(t)
                        if t >= 2:
                            banks[3].wait(dve, ("hT", t - 2, 1))
                        signal("hn").mark(ts(hn[0:n, t % 2, :], X[0:n, t, :], nrms[0:n, t:t + 1], None, ALU.mult), t)
                    if t >= 1:
                        n = rows(t - 1)
                        for h in range(2):
                            b = banks[2 + h]
                            b.wait(dve, ("hT", t - 1, h))
                            b.release(tt(hT[:, 4 * h:4 * h + 4, tok(t - 1)], heads(b.ap, 4, P)[:, :, 0:n],
                                         bc(g1[:, 4 * h:4 * h + 4], n), ALU.mult), ("hT", t - 1, h))
                signal("rope").wait(dve, "in")
                for g in range(16):
                    i, half = g // 2, g % 2
                    cols = slice(half * HALF, half * HALF + HALF)
                    b = banks[g % 2]
                    b.wait(dve, ("qk", g))
                    signal("xsw").wait(dve, g)
                    tt(rot1[:, g % 2, :], b.ap[:, 0:HALF], rope[:, 0, cols], ALU.mult)
                    b.release(tt(rot2[:, g % 2, :], xsw[:, g % 2, :], rope[:, 1, cols], ALU.mult), ("qk", g))
                    b.wait_freed(dve, ("qk", g))
                    signal("qk").mark(tt(qk[:, i, cols], rot1[:, g % 2, :], rot2[:, g % 2, :], ALU.add), g)

                signal("vectors").wait(dve, "in")

                def onT_out(t):
                    n = rows(t)
                    banks[3].wait(dve, ("onT", t))
                    banks[3].release(tt(onT[:, :, tok(t)], heads(bk[3], 4, P)[:, :, 0:n], bc(gnT, n), ALU.mult), ("onT", t))

                for t in range(NT):
                    n = rows(t)
                    sfx = "" if t < SAMPLE else "_s"
                    if t >= 2:
                        banks[7].wait(dve, ("kv", t - 2))
                    banks[2].wait(dve, ("ktok", t))
                    banks[2].release(tt(heads(ktok[0:n, t % 2, :], 4, DK), heads(bk[2][0:n, :], 4, DK), bc(C("kdec" + sfx, n), DK), ALU.mult), ("ktok", t))
                    banks[4].wait(dve, ("scores", t))
                    banks[4].release(tt(sc[0:n, t % 2, 0:4 * n], bk[4][0:n, 0:4 * n], C("decay" + sfx, n), ALU.mult), ("scores", t))
                    signal("erg").wait(dve, t)
                    e = erg[0:n, t % 2, :]
                    step(ts(e, e, 1.0, None, ALU.add))
                    step(v.reciprocal(e, e))
                    banks[1].release(tt(rgs[0:n, t % 2, :], bk[1][0:n, :], e, ALU.mult), ("rg", t))
                    o, c = ret_o[0:n], ret_c[0:n]
                    banks[6].wait(dve, ("inter", t))
                    banks[6].release(tt(heads(o, 4, DV), heads(bk[6][0:n, :], 4, DV), bc(C("qdec" + sfx, n), DV), ALU.mult), ("inter", t))
                    banks[6].wait_freed(dve, ("inter", t))
                    banks[5].wait(dve, ("intra", t))
                    banks[5].release(tt(o, o, bk[5][0:n, :], ALU.add), ("intra", t))
                    if t < SAMPLE:
                        banks[7].wait(dve, ("kv", t))
                        for h in range(H_RET):
                            hs = slice(h * DV, (h + 1) * DV)
                            last = stt(S_ret[:, hs], S_ret[:, hs], G[h] ** P, bk[7][:, hs], ALU.mult, ALU.add)
                        banks[7].release(last, ("kv", t))
                    else:
                        for h in range(H_RET):
                            for q in range(2):
                                b = banks[(7, 4)[q]]
                                b.wait(dve, ("kvs", h, q))
                                sl = natR[:, 4 * q:4 * q + 4, h, :]
                                b.release(stt(sl, sl, G[h] ** DEC_S, heads(b.ap, 4, DV), ALU.mult, ALU.add), ("kvs", h, q))
                    banks[5].wait_freed(dve, ("intra", t))
                    step(v.tensor_reduce(gsum[0:n], heads(o, 4, DV), AX.X, ALU.add))
                    step(ts(gsum[0:n], gsum[0:n], 1.0 / DV, None, ALU.mult))
                    step(tt(heads(c, 4, DV), heads(o, 4, DV), bc(gsum[0:n], DV), ALU.subtract))
                    step(tt(o, c, c, ALU.mult))
                    step(v.tensor_reduce(gvar[0:n], heads(o, 4, DV), AX.X, ALU.add))
                    signal("var").mark(ts(gvar[0:n], gvar[0:n], 1.0 / DV, EPS, ALU.mult, ALU.add), ("gn", t))
                    signal("var").wait(dve, ("gn", t))
                    refine(("gn", t), n, gvar, grs, gnt, grms)
                    step(tt(heads(c, 4, DV), heads(c, 4, DV), bc(grms[0:n], DV), ALU.mult))
                    if t >= 1:
                        onT_out(t - 1)
                    banks[1].wait_freed(dve, ("rg", t))
                    signal("gated").mark(tt(ret_q[0:n], c, rgs[0:n, t % 2, :], ALU.mult), t)
                onT_out(SAMPLE)

                step(v.memset(S_ssm, 0.0))
                for par in range(2):
                    step(v.memset(xr[:, par, 0:CONV_K - 1], 0.0))
                signal("state_zero").mark(v.memset(conv[64:128, 9, :], 0.0), "ssm")
                step(v.memset(conv[0:64, 10, :], 0.0))

                def samp(ap, w):
                    return ap.rearrange("p (b r) -> p b r", b=DEC_B, r=w)

                for g in range(NCT + 1):
                    if g == 2:
                        signal("head_vectors").wait(dve, "in")
                        banks[3].wait(dve, ("dt",))
                        dps = bk[3][:, 0:NT * H_SSD].rearrange("p (t h) -> p t h", t=NT)
                        tt(dts[:, 0:SAMPLE, :], dps[:, 0:SAMPLE, :], bm(dtb, SAMPLE), ALU.add)
                        banks[3].release(tt(dts[0:NSAMP, SAMPLE, :], dps[0:NSAMP, SAMPLE, :], dtb[0:NSAMP], ALU.add), ("dt",))
                        banks[3].wait_freed(dve, ("dt",))
                        step(ts(dt1, dts, -1.0, None, ALU.mult))
                        signal("sp").mark(tt(dt1, dt1, dts, ALU.min), "arg")
                    if g == 4:
                        signal("spa").wait(dve, "e")
                        signal("sp").mark(ts(dt1, dt2, 1.0, None, ALU.add), "u")
                        signal("sp").wait(dve, "u")
                        step(ts(cum, dt1, -1.0, 1e-30, ALU.add, ALU.max))
                        step(v.reciprocal(cum, cum))
                        step(tt(cum, cum, dt2, ALU.mult))
                    if g == 6:
                        signal("spa").wait(dve, "ln")
                        step(tt(cum, cum, dt3, ALU.mult))
                        step(stt(dt3, dt1, 1.0, dt2, ALU.is_equal, ALU.mult))
                        step(tt(cum, cum, dt3, ALU.add))
                        step(stt(dts, dts, 0.0, cum, ALU.max, ALU.add))
                        signal("acoef").wait(dve, 0)
                        step(ts(acoef, acoef, -1.0, None, ALU.mult))
                        step(tt(dta, dts, bm(acoef, NT), ALU.mult))
                        step(v.memset(cum, 0.0))
                        signal("dta").mark(v.memset(cend, 0.0), 0)
                    if g == 9:
                        banks[3].wait(dve, ("cum",))
                        signal("dta").wait(dve, 0)
                        cps = bk[3][:, 0:NT * 32].rearrange("p (t h) -> p t h", t=NT)
                        for dst, off in ((cum, 0), (cend, 16)):
                            cp(dst[:, 0:SAMPLE, :], cps[:, 0:SAMPLE, off:off + 16])
                            last = cp(dst[0:NSAMP, SAMPLE, :], cps[0:NSAMP, SAMPLE, off:off + 16])
                        banks[3].release(last, ("cum",))
                        banks[3].wait_freed(dve, ("cum",))
                        ts(ncum, cum, -1.0, None, ALU.mult)
                        signal("decays").mark(tt(wend, cend, cum, ALU.subtract), "args")
                    if g < NCT:
                        for h in range(2):
                            banks[h].wait_freed(dve, ("x", g, h))
                        pr, out = xr[:, g % 2, :], cb_[:, g % 2, :]
                        sa = samp(pr[:, 3 + SEQ:], DEC_S + 3)
                        so = samp(out[:, SEQ:TOK], DEC_S)
                        if g >= 2:
                            signal("conv").wait(dve, g - 2)
                        for j in range(CONV_K):
                            w = conv_wT[:, g, j:j + 1]
                            if j == 0:
                                ts(out[:, 0:SEQ], pr[:, 0:SEQ], w, conv_bT[:, g:g + 1], ALU.mult, ALU.add)
                                last = ts(so, sa[:, :, 0:DEC_S], w, conv_bT[:, g:g + 1], ALU.mult, ALU.add)
                            else:
                                stt(out[:, 0:SEQ], pr[:, j:j + SEQ], w, out[:, 0:SEQ], ALU.mult, ALU.add)
                                last = stt(so, sa[:, :, j:j + DEC_S], w, so, ALU.mult, ALU.add)
                            if j < CONV_K - 1:
                                step(last)
                        signal("lin").mark(last, g)
                    if g >= 1:
                        k = g - 1
                        signal("ce").wait(dve, k)
                        e, c = ce[:, k % 2, :], cb_[:, k % 2, :]
                        step(ts(e, e, 1.0, None, ALU.add))
                        step(v.reciprocal(e, e))
                        if k < 9:
                            last = tt(conv[:, k, :], c, e, ALU.mult)
                        else:
                            tt(conv[0:64, 9, :], c[0:64], e[0:64], ALU.mult)
                            last = tt(conv[64:128, 10, :], c[64:128], e[64:128], ALU.mult)
                        signal("conv").mark(last, k)

                def yT_out(t):
                    n = rows(t)
                    if t == 0:
                        for key in ("retp", "convp", "convs"):
                            signal("out_" + key).wait(dve, "out")
                    for h in range(2):
                        b = banks[(2 if t < SAMPLE else 5) + h]
                        b.wait(dve, ("yT", t, h))
                        b.release(tt(yT[:, 4 * h:4 * h + 4, tok(t)], heads(b.ap, 4, P)[:, :, 0:n], bc(sngT[:, 4 * h:4 * h + 4], n), ALU.mult), ("yT", t, h))

                signal("decayed").wait(dve, 0)
                signal("out_retp").wait(dve, "out")
                signal("head_vectors").wait(dve, "in")
                step(v.memset(btz, 0.0))
                for t in range(NT):
                    n = rows(t)
                    if t:
                        banks[3].wait(dve, ("yin", t - 1, 1))
                        signal("wx").wait(dve, t - 1)
                    for h in range(2):
                        b = banks[2 + h]
                        b.wait(dve, ("xsT", t, h))
                        signal("xs").wait(dve, (t, h))
                        b.release(tt(heads(xdt[0:n, 512 * h:512 * h + 512], 8, 64), heads(b.ap[0:n, :], 8, 64), bc(dts[0:n, t, 8 * h:8 * h + 8], 64), ALU.mult), ("xsT", t, h))
                    banks[4].wait(dve, ("cb", t))
                    if t:
                        banks[7].wait(dve, ("bx", t - 1))
                    for g in range(2):
                        last = cp(btz[0:n, g, 64 * g:64 * g + 64], bk[4][0:n, 256 + 64 * g:320 + 64 * g])
                    signal("btz").mark(last, t)
                    for r in range(4):
                        b = banks[5 + r % 2]
                        b.wait_freed(dve, ("seg", t, r))
                        w = wl[0:n, 4 * r * n:4 * (r + 1) * n].rearrange("p (h m) -> p h m", h=4)
                        last = tt(w, w, bm(bk[4][0:n, (r // 2) * n:(r // 2 + 1) * n], 4), ALU.mult)
                    banks[4].release(last, ("cb", t))
                    if t:
                        yT_out(t - 1)
                    if t == SAMPLE:
                        signal("out_ssmp").wait(dve, "out")
                    for h in range(2):
                        hs = slice(512 * h, 512 * h + 512)
                        signal("ez").wait(dve, (t, h))
                        step(ts(ez[0:n, hs], ez[0:n, hs], 1.0, None, ALU.add))
                        step(v.reciprocal(ez[0:n, hs], ez[0:n, hs]))
                        banks[h].release(tt(zs[0:n, hs], bk[h][0:n, :], ez[0:n, hs], ALU.mult), ("z", t, h))
                    if t == SAMPLE:
                        for g in range(2):
                            if g:
                                banks[4].wait(dve, ("bxs", 3))
                            else:
                                signal("btz").wait(dve, t)
                                banks[1].wait_freed(dve, ("z", t, 1))
                            signal("bexp").mark(tt(heads(bexp[0:n], 8, 64), bm(btz[0:n, g, 64 * g:64 * g + 64], 8), bc(C("seqcol", n), 64), ALU.mult), g)
                            for c in range(4 * g, 4 * g + 4):
                                b = banks[(7, 4)[c % 2]]
                                if c == 0:
                                    banks[7].wait_freed(dve, ("e8",))
                                old = natS[:, :, c % 4, c // 4, :]
                                step(tt(old, old, bc(E8[:, c, :], 64), ALU.mult))
                                b.wait(dve, ("bxs", c))
                                b.release(tt(old, old, heads(b.ap, 8, 64), ALU.add), ("bxs", c))
                    if t:
                        banks[3].wait(dve, ("yT", t - 1, 1))
                    for g in range(2):
                        gs = slice(512 * g, 512 * g + 512)
                        banks[5 + g].wait(dve, ("yst", t, g))
                        banks[5 + g].release(tt(heads(yb[0:n, gs], 8, 64), heads(bk[5 + g][0:n, :], 8, 64), bc(ecum[0:n, t, 8 * g:8 * g + 8], 64), ALU.mult), ("yst", t, g))
                    for g in range(2):
                        gs = slice(512 * g, 512 * g + 512)
                        banks[5 + g].wait_freed(dve, ("yst", t, g))
                        banks[2 + g].wait(dve, ("yin", t, g))
                        banks[2 + g].release(tt(yb[0:n, gs], yb[0:n, gs], bk[2 + g][0:n, :], ALU.add), ("yin", t, g))
                    if t < SAMPLE:
                        banks[7].wait(dve, ("bx", t))
                        for g in range(2):
                            gp = slice(64 * g, 64 * g + 64)
                            last = tt(heads(S_ssm[gp], 8, 64), heads(S_ssm[gp], 8, 64), bc(dec[gp, t, 8 * g:8 * g + 8], 64), ALU.mult)
                        step(last)
                        banks[7].release(tt(S_ssm, S_ssm, bk[7], ALU.add), ("bx", t))
                    signal("xsd").wait(dve, t)
                    banks[3].wait_freed(dve, ("yin", t, 1))
                    signal("ylin").mark(tt(yb[0:n], yb[0:n], xs[0:n], ALU.add), t)
                    signal("ylin").wait(dve, t)
                    banks[1].wait_freed(dve, ("z", t, 1))
                    signal("yz").mark(tt(yb[0:n], yb[0:n], zs[0:n], ALU.mult), t)
                    signal("ysq").wait(dve, t)
                    signal("var").mark(ts(yvar[0:n], ysum[0:n], 1.0 / 512, EPS, ALU.mult, ALU.add), ("y", t))
                    signal("var").wait(dve, ("y", t))
                    refine(("y", t), n, yvar, yrs, ynt, yrms)
                    signal("y").mark(tt(heads(yb[0:n], 2, 512), heads(yb[0:n], 2, 512), bc(yrms[0:n], 512), ALU.mult), t)
                yT_out(SAMPLE)

                for g in range(32):
                    c, half = (g // 2) % 8, g % 2
                    cols = slice(half * HALF, half * HALF + HALF)
                    banks[g % 2].wait_freed(dve, ("gate", g))
                    e = ge[:, g % 2, :]
                    step(ts(e, e, 1.0, None, ALU.add))
                    step(v.reciprocal(e, e))
                    b = banks[2 + g % 2]
                    b.wait(dve, ("branch", g))
                    if g < 16:
                        b.release(tt(mT[:, c, cols], e, b.ap[:, 0:HALF], ALU.mult), ("branch", g))
                    else:
                        b.release(tt(mix2, e, b.ap[:, 0:HALF], ALU.mult), ("branch", g))
                        b.wait_freed(dve, ("branch", g))
                        signal("mix").mark(tt(mT[:, c, cols], mT[:, c, cols], mix2, ALU.add), g)

                signal("x_spilled").wait(dve, "in")
                for key in ("ssmp", "ssms"):
                    signal("out_" + key).wait(dve, "out")

                def tT_out(t):
                    n = rows(t)
                    if t >= 2:
                        banks[0].wait(dve, ("logits", t - 2))
                    for h in range(2):
                        b = banks[2 + h]
                        b.wait(dve, ("tT", t, h))
                        b.release(tt(tT[:, t % 2, 4 * h:4 * h + 4, 0:n], heads(b.ap, 4, P)[:, :, 0:n], bc(g2[:, 4 * h:4 * h + 4], n), ALU.mult), ("tT", t, h))

                for t in range(NT):
                    n, one = rows(t), slice(t, t + 1)
                    for h in range(2):
                        b = banks[4 + (2 * t + h) % 4]
                        b.wait(dve, ("wo", t, h))
                        xx = X[0:n, t, 512 * h:512 * h + 512]
                        b.release(tt(xx, xx, b.ap[0:n, :], ALU.add), ("wo", t, h))
                        if t and h == 0:
                            tT_out(t - 1)
                    signal("sq2").wait(dve, t)
                    signal("var").mark(ts(nvar2[0:n, one], ssq2[0:n, one], 1.0 / D_MODEL, EPS, ALU.mult, ALU.add), ("n2", t))
                    signal("var").wait(dve, ("n2", t))
                    refine(("n2", t), n, nvar2[:, one], nrs2[:, one], nnt2[:, one], nrms2[:, one])
                    signal("xn").mark(ts(xn[0:n, t, :], X[0:n, t, :], nrms2[0:n, one], None, ALU.mult), t)
                tT_out(SAMPLE)

                for ap in (glog, elog, rank, hit[:, NT, :]):
                    step(v.memset(ap, 0.0))
                banks[1].wait(dve, ("router",))
                rps = bk[1][:, 0:NT * 20].rearrange("p (t e) -> p t e", t=NT)
                for dst, a, z in ((glog, 0, 4), (elog, 4, 20)):
                    cp(dst[:, 0:SAMPLE, :], rps[:, 0:SAMPLE, a:z])
                    last = cp(dst[0:NSAMP, SAMPLE, :], rps[0:NSAMP, SAMPLE, a:z])
                banks[1].release(last, ("router",))
                banks[1].wait_freed(dve, ("router",))

                def top(val, best, back, scratch, idx, hot):
                    n = val.shape[2]
                    step(v.tensor_reduce(best, val, AX.X, ALU.max))
                    step(tt(scratch, val, bc(best, n), ALU.is_equal))
                    step(tt(scratch, scratch, bm(C(back), NT), ALU.mult))
                    step(v.tensor_reduce(idx, scratch, AX.X, ALU.min))
                    step(tt(hot, bm(C(back), NT), bc(idx, n), ALU.is_equal))

                top(glog, gmax, "back4", r4b, gidx, r4a)
                step(ts(r4b, r4a, 1.0, BIG, ALU.subtract, ALU.mult))
                step(tt(ra.rearrange("p t (g e) -> p (t g) e", g=N_GRP), elog.rearrange("p t (g e) -> p (t g) e", g=N_GRP),
                        bc(r4b.rearrange("p t g -> p (t g)"), EXP_PG), ALU.add))
                top(ra, m1, "back16", rb, i1, oh1)
                step(stt(ra, oh1, -BIG, ra, ALU.mult, ALU.add))
                top(ra, m2, "back16", rb, i2, oh2)
                hits = hit[:, 0:NT, :]
                step(tt(hits, oh1, oh2, ALU.add))
                signal("hit").mark(tt(hits, hits, bc(C("valid"), N_EXP), ALU.mult), 0)
                signal("route").mark(tt(r4a, glog, bc(gmax, N_GRP), ALU.subtract), "gd")
                signal("route").mark(tt(rt1, m2, m1, ALU.subtract), "ed")
                signal("routea").wait(dve, "g")
                step(v.tensor_reduce(gden, r4b, AX.X, ALU.add))
                step(v.reciprocal(gden, gden))
                signal("routea").wait(dve, "e")
                step(ts(rt3, rt2, 1.0, None, ALU.add))
                step(v.reciprocal(rt3, rt3))
                step(tt(w1, rt3, gden, ALU.mult))
                step(tt(w2, w1, rt2, ALU.mult))
                banks[0].wait(dve, ("rank",))
                kps = bk[0][:, 0:80].rearrange("p (t e) -> p t e", t=NT)
                cp(rank[:, 0:SAMPLE, :], kps[:, 0:SAMPLE, :])
                cp(rank[0:NSAMP, SAMPLE, :], kps[0:NSAMP, SAMPLE, :])
                banks[0].release(cp(tot, bk[0][:, 80:96]), ("rank",))
                banks[0].wait_freed(dve, ("rank",))
                step(ts(otile, tot, float(MAIN_CAP), None, ALU.is_gt))
                for k in range(1, (TOK - MAIN_CAP - 1) // CAP + 1):
                    step(stt(otile, tot, float(MAIN_CAP + CAP * k), otile, ALU.is_gt, ALU.add))
                step(cp(oscan, otile))
                for k in (1, 2, 4, 8):
                    step(cp(oend, oscan))
                    step(tt(oscan[:, k:], oend[:, k:], oend[:, 0:N_EXP - k], ALU.add))
                step(tt(obase, oscan, otile, ALU.subtract))
                step(ts(oend, obase, float(CAP), float(MAIN * CAP - MAIN_CAP), ALU.mult, ALU.add))
                step(tt(ra, rank, bm(C("slot0"), NT), ALU.add))
                step(tt(rb, rank, bm(oend, NT), ALU.add))
                step(tt(ra, ra, rb, ALU.subtract))
                step(stt(ra, rank, float(MAIN_CAP), ra, ALU.is_lt, ALU.mult))
                step(tt(slot_e, ra, rb, ALU.add))
                for c, oh in enumerate((oh1, oh2)):
                    step(tt(ra, oh, slot_e, ALU.mult))
                    step(v.tensor_reduce(slots_f[:, c, :], ra, AX.X, ALU.add))
                signal("slots").mark(cp(slot_i[:], slots_f.rearrange("p c t -> p (c t)")), 0)
                step(tt(ov_a, bc(C("overno"), N_EXP), bm(obase, OVER), ALU.is_ge))
                step(tt(ov_b, bc(C("overno"), N_EXP), bm(oscan, OVER), ALU.is_lt))
                step(tt(ov_a, ov_a, ov_b, ALU.mult))
                step(tt(ov_a, ov_a, bm(C("expno"), OVER), ALU.mult))
                step(v.tensor_reduce(ov_c, ov_a, AX.X, ALU.add))
                cp(over_i[:, OVER:OVER + 1], oscan[:, N_EXP - 1:N_EXP])
                signal("slots").mark(cp(over_i[:, 0:OVER], ov_c), "over")

                def act_tile(s, j):
                    dve.sem_clear(moe_chain)
                    dve.wait_ge(sig_e, j + 1)
                    ts(fe, fe, 1.0, None, ALU.add).then_inc(moe_chain, 1)
                    dve.wait_ge(moe_chain, 1)
                    v.reciprocal(fe, fe).then_inc(moe_chain, 1)
                    dve.wait_ge(moe_chain, 2)
                    if not isinstance(j, int) or j > 1:
                        dve.wait_ge(act_T, j - 1)
                    tt(fa[:, s, :], bk[0], fe, ALU.mult).then_inc(moe_chain, 1)
                    dve.wait_ge(moe_chain, 3)
                    tt(fa[:, s, :], fa[:, s, :], bk[1], ALU.mult).then_inc(acted, 1)

                def copy_rows(s, j):
                    dve.wait_ge(x_T, j + 1)
                    if not isinstance(j, int) or j > 1:
                        dve.wait_ge(gate_up, j - 1)
                    for h in range(2):
                        last = tt(xsT[:, s, 4 * h:4 * h + 4, :], heads(bk[2 + h], 4, P), bc(g2[:, 4 * h:4 * h + 4], P), ALU.mult)
                    last.then_inc(x_Tc, 1)

                def activate_tiles(first, count):
                    copy_rows(0, first)
                    copy_rows(1, first + 1)
                    act_tile(0, first)
                    with dve.Fori(0, (count - 2) // 2) as t2:
                        for q in range(2):
                            s = 1 - q
                            act_tile(s, t2 * 2 + (first + 1 + q))
                            copy_rows(1 - s, t2 * 2 + (first + 2 + q))
                    act_tile(1, first + count - 1)

                activate_tiles(0, MAIN)
                signal("slots").wait(dve, "over")
                with dve.If(dve.value_load(over_i[0:1, OVER:OVER + 1], min_val=0, max_val=OVER) > 0):
                    activate_tiles(MAIN, OVER)

                for t in range(NT):
                    n = rows(t)
                    for c, w in enumerate((w1, w2)):
                        dve.wait_ge(gathered[c * NT + t], L * 16 + 16)
                        last = stt(X[0:n, t, :], got[0:n, c * NT + t, :], w[0:n, t:t + 1], X[0:n, t, :], ALU.mult, ALU.add)
                        if c == 0:
                            step(last)
                    signal("combined").mark(last, t)
                input_rms("next", step)
                meet(dve, L)

            dve.wait_ge(final_loaded, 16)
            for t in range(NT):
                n = rows(t)
                last = stt(xn[0:n, t, :], X[0:n, t, :], nrms[0:n, t:t + 1], gf[0:n], ALU.mult, ALU.mult)
            last.then_inc(final_made, 1)

        @block.gpsimd
        def _(pool):
            g_ = nc.gpsimd
            pool.wait_ge(setup_made, 1)
            pool.wait_ge(slot_loaded[1], 16)
            for i in range(TILES):
                pool.dma_start(slot_in[i * P:(i + 1) * P, :].rearrange("p (c x) -> p c x", c=8), bm(zero[:], 8)).then_inc(zeroed, 16)
            for i in range(MAIN, TILES):
                pool.dma_start(slot_out[i * P:(i + 1) * P, :].rearrange("p (c x) -> p c x", c=8), bm(zero[:], 8)).then_inc(zeroed, 16)
            pool.wait_ge(zeroed, 16 * (TILES + OVER))
            with pool.Fori(0, DEPTH) as L:
                signal("qk").wait(pool, 15)
                seqrow = C("seqrow").rearrange("p (b m) -> p b m", b=DEC_B)
                for h in range(H_RET):
                    signal("qexp").mark(g_.tensor_tensor(qexp[:, h, :].rearrange("p (b m) -> p b m", b=DEC_B), bm(qk[:, h, tok(SAMPLE)], DEC_B), seqrow, ALU.mult), h)
                banks[0].wait_freed(pool, ("v", SAMPLE))
                for h in range(H_RET):
                    for q in range(2):
                        if h:
                            banks[(7, 4)[q]].wait(pool, ("kvs", h - 1, q))
                        signal("vexp").mark(g_.tensor_tensor(vexp[0:NSAMP, 4 * q:4 * q + 4, :], bm(vt[0:NSAMP, SAMPLE % 2, h * DV:(h + 1) * DV], 4),
                                                             bc(C("seqcol", NSAMP)[:, 4 * q:4 * q + 4], DV), ALU.mult), (h, q))
                signal("gated").wait(pool, SAMPLE)
                for g in range(NCT):
                    for h in range(2):
                        banks[h].wait_freed(pool, ("x", g, h))
                    g_.tensor_copy(cvo[:, g, 0:3], xr[:, g % 2, SEQ:SEQ + 3])
                    signal("cvo").mark(g_.tensor_copy(cvo[:, g, 3:27].rearrange("p (b r) -> p b r", b=DEC_B),
                                                      xr[:, g % 2, 3 + SEQ:].rearrange("p (b r) -> p b r", b=DEC_B)[:, :, DEC_S:]), g)
                signal("head_vectors").wait(pool, "in")
                signal("dta").wait(pool, 0)
                signal("decayed").wait(pool, 0)
                signal("conv").wait(pool, NCT - 1)
                for q in range(3):
                    banks[4 + q].wait(pool, ("cvo", q))
                for t in range(NT):
                    n = rows(t)

                    def udo(r):
                        if r >= 2 or t:
                            banks[5 + r % 2].wait(pool, ("seg", t, r - 2) if r >= 2 else ("seg", t - 1, r + 2))
                        m = C("upto" if t < SAMPLE else "upto_s", n)
                        signal("ud").mark(g_.tensor_tensor(ud[0:n, r % 2, 0:4 * n].rearrange("p (h m) -> p h m", h=4), bm(m, 4),
                                                           bc(dta[0:n, t, 4 * r:4 * r + 4], n), ALU.mult), (t, r))
                    for r in range(4):
                        udo(r)
                    for h in range(2):
                        banks[2 + h].wait_freed(pool, ("xsT", t, h))
                    if t:
                        banks[7].wait(pool, ("bx", t - 1))
                    signal("wx").mark(g_.tensor_tensor(wx[0:n].rearrange("p (h w) -> p h w", h=H_SSD), xdt[0:n].rearrange("p (h w) -> p h w", h=H_SSD),
                                                       bc(wend[0:n, t, :], 64), ALU.mult), t)
                    signal("xsd").mark(g_.tensor_tensor(xs[0:n].rearrange("p (h w) -> p h w", h=H_SSD), xs[0:n].rearrange("p (h w) -> p h w", h=H_SSD),
                                                        bc(dskip[0:n], 64), ALU.mult), t)
                    if t == SAMPLE:
                        banks[3].wait(pool, ("yin", t - 1, 1))
                        for g in range(2):
                            signal("czexp").mark(g_.tensor_tensor(czexp[:, 512 * g:512 * g + 512].rearrange("p (b m) -> p b m", b=DEC_B),
                                                                  bm(conv[:, 9 + g, tok(t)], DEC_B), seqrow, ALU.mult), g)
                        banks[6].wait(pool, ("seg", t, 3))
                        signal("dtx").mark(g_.tensor_copy(dtx[0:n].rearrange("p (h w) -> p h w", h=H_SSD), bc(dta[0:n, t, :], 64)), 0)
                signal("slots").wait(pool, 0)
                signal("xn").wait(pool, NT - 1)
                for c in range(2):
                    for t in range(NT):
                        n = rows(t)
                        g_.indirect_dma_start(slot_in, bass.IndirectOffsetOnAxis(ap=slot_i[0:n, c * NT + t:c * NT + t + 1], axis=0),
                                              xn[0:n, t, :], None).then_inc(scattered, 16)
                pool.wait_ge(scattered, L * (32 * NT) + 32 * NT)
                pool.sem_inc(aside, 1)
                signal("slots").wait(pool, "over")
                signal("rows_ready").mark(g_.memset(mark_row, 0.0), "all")
                for s in range(2):
                    pool.wait_ge(out_stored[s], 16 + 16 * (MAIN // 2))
                with pool.If(pool.value_load(over_i[0:1, OVER:OVER + 1], min_val=0, max_val=OVER) > 0):
                    for s in range(2):
                        pool.wait_ge(out_stored[s], 16 + 16 * (TILES // 2))
                for t in range(NT):
                    n = rows(t)
                    for c in range(2):
                        g_.indirect_dma_start(got[0:n, c * NT + t, :], None, slot_out,
                                              bass.IndirectOffsetOnAxis(ap=slot_i[0:n, c * NT + t:c * NT + t + 1], axis=0)).then_inc(gathered[c * NT + t], 16)
                meet(pool, L)

    plan["names"] = list(signals)


_INS = ["x_prompt", "x_sample", "state_ret", "state_ssm", "state_conv", "ln1_g", "w_in", "ret_gn_g", "w_ret_out",
        "conv_w", "conv_b", "dt_bias", "a_log", "d_skip", "ssd_norm_g", "w_ssd_out", "w_o", "ln2_g",
        "w_router_group", "w_router_expert", "w_e_gate", "w_e_up", "w_e_down", "lnf_g"]
_OUTS = [(1, SEQ, D_MODEL), (DEC_B, DEC_S, D_MODEL), (DEPTH, 1, H_RET, DK, DV), (DEPTH, 1, H_SSD, P_SSD, N_SSD),
         (DEPTH, 1, CONV_K - 1, CONV_DIM), (DEPTH, DEC_B, H_RET, DK, DV), (DEPTH, DEC_B, H_SSD, P_SSD, N_SSD),
         (DEPTH, DEC_B, CONV_K - 1, CONV_DIM)]


def kernel(**inputs):
    import numpy as _np
    import concourse.bacc as _bacc
    from concourse import mybir as _mybir
    from concourse.bass_utils import run_bass_kernel_spmd as _run

    arrays = {f"in_{name}": _np.ascontiguousarray(inputs[name]) for name in _INS}
    arrays["in_table"] = _np.concatenate(list(constants().values()), 1)
    plan = {}
    for _ in range(2):
        nc = _bacc.Bacc("TRN2", target_bir_lowering=False, num_devices=1)
        args = [nc.dram_tensor(n, a.shape, _mybir.dt.from_np(a.dtype), kind="ExternalInput").ap() for n, a in arrays.items()]
        args += [nc.dram_tensor(f"out_{i}", shape, _mybir.dt.float32, kind="ExternalOutput").ap() for i, shape in enumerate(_OUTS)]
        build(nc, plan, *args)
    r = _run(nc, [arrays], core_ids=[0])
    return tuple(r.results[0][f"out_{i}"] for i in range(len(_OUTS)))
```
